# Optimizing a Trainium2 kernel written in Bass

```python
import jax, jax.numpy as jnp
from jax import lax
import numpy as np

D_MODEL = 1024
BATCH = 1
SEQ = 128
DEPTH = 2
DEC_BATCH = 1
DEC_SEQ = 256
PAST_LEN = 128

GRID_W = 64
D_MIX = D_MODEL
ATTN_WIDTH = D_MIX // 2
POOL_WIDTH = D_MIX - ATTN_WIDTH
HEAD_DIM = 64
N_HEADS = ATTN_WIDTH // HEAD_DIM
N_KV_HEADS = 2
KV_WIDTH = N_KV_HEADS * HEAD_DIM
POOL_WINDOWS = (2, 4, 8, 16)
N_POOL_GROUPS = len(POOL_WINDOWS)
POOL_GC = POOL_WIDTH // N_POOL_GROUPS
IN_COLS = ATTN_WIDTH + 2 * KV_WIDTH + POOL_WIDTH
D_FF = 2816
N_EXPERTS = 8
TOP_K = 2
D_FF_EXPERT = 2816
N_DENSE = (DEPTH + 1) // 2
N_MOE = DEPTH // 2
Q_BLOCK = 128
ROPE_THETA = 10000.0
EPS = 1e-6

kernel_name = "hybrid_pool_gqa_prefix_diffusion_step"

def _rms_norm(x, w):
    xf = x.astype(jnp.float32)
    y = xf * lax.rsqrt(jnp.mean(xf * xf, axis=-1, keepdims=True) + EPS)
    return (y * w.astype(jnp.float32)).astype(x.dtype)

def _axial_rope(n):
    rows = n // GRID_W
    row = jnp.repeat(jnp.arange(rows, dtype=jnp.float32), GRID_W)
    col = jnp.tile(jnp.arange(GRID_W, dtype=jnp.float32), rows)
    nf = HEAD_DIM // 4
    inv = ROPE_THETA ** (-jnp.arange(nf, dtype=jnp.float32) / nf)
    ang = jnp.stack([row[:, None] * inv, col[:, None] * inv], axis=1)
    return jnp.cos(ang), jnp.sin(ang)

def _apply_rope(x, cos, sin):
    nf = HEAD_DIM // 4
    xr = x.reshape(x.shape[:-1] + (2, 2, nf))
    a, b = xr[..., 0, :], xr[..., 1, :]
    cs = cos.astype(x.dtype)[None, :, None]
    sn = sin.astype(x.dtype)[None, :, None]
    out = jnp.stack([a * cs - b * sn, b * cs + a * sn], axis=-2)
    return out.reshape(x.shape)

def _attend(q, k, v):
    B, Nq, H, D = q.shape
    KV = k.shape[2]
    G = H // KV
    scale = 1.0 / np.sqrt(D)
    qb = q.reshape(B, Nq // Q_BLOCK, Q_BLOCK, KV, G, D).transpose(1, 0, 2, 3, 4, 5)

    def block(qi):
        s = jnp.einsum('bqkgd,bskd->bkgqs', qi, k, preferred_element_type=jnp.float32) * scale
        p = jax.nn.softmax(s, axis=-1).astype(v.dtype)
        return jnp.einsum('bkgqs,bskd->bqkgd', p, v)

    o = lax.map(block, qb)
    return o.transpose(1, 0, 2, 3, 4, 5).reshape(B, Nq, H * D)

def _multiscale_pool(u, pool_w, pool_scale):
    B, N, _ = u.shape
    uf = u.reshape(B, N, N_POOL_GROUPS, POOL_GC).astype(jnp.float32)
    cs = jnp.concatenate([jnp.zeros((B, 1, N_POOL_GROUPS, POOL_GC), jnp.float32),
                          jnp.cumsum(uf, axis=1)], axis=1)
    t = jnp.arange(N)
    means = []
    for g, w in enumerate(POOL_WINDOWS):
        lo = jnp.clip(t - w // 2, 0, N)
        hi = jnp.clip(t + w // 2, 0, N)
        s = cs[:, hi, g] - cs[:, lo, g]
        means.append(s / (hi - lo).astype(jnp.float32)[None, :, None])
    d = (jnp.stack(means, axis=2) - uf).astype(u.dtype)
    y = jnp.einsum('bngc,gcd->bngd', d, pool_w)
    return y.reshape(B, N, POOL_WIDTH) * pool_scale

def _mixer(h, w_in, w_o, q_norm_w, k_norm_w, pool_w, pool_scale, rope, k_ctx, v_ctx):
    B, N, _ = h.shape
    proj = h @ w_in
    q = proj[..., :ATTN_WIDTH].reshape(B, N, N_HEADS, HEAD_DIM)
    k = proj[..., ATTN_WIDTH:ATTN_WIDTH + KV_WIDTH].reshape(B, N, N_KV_HEADS, HEAD_DIM)
    v = proj[..., ATTN_WIDTH + KV_WIDTH:ATTN_WIDTH + 2 * KV_WIDTH].reshape(B, N, N_KV_HEADS, HEAD_DIM)
    u = proj[..., ATTN_WIDTH + 2 * KV_WIDTH:]
    q = _rms_norm(q, q_norm_w)
    k = _rms_norm(k, k_norm_w)
    if rope is None:
        attn = _attend(q, k, v)
    else:
        q = _apply_rope(q, *rope)
        keys = jnp.concatenate([_apply_rope(k, *rope), k_ctx], axis=1)
        vals = jnp.concatenate([v, v_ctx], axis=1)
        attn = _attend(q, keys, vals)
    pool = _multiscale_pool(u, pool_w, pool_scale)
    out = jnp.concatenate([attn, pool], axis=-1) @ w_o
    return out, k, v

def _swiglu(h, w1, w3, w2):
    return (jax.nn.silu(h @ w1) * (h @ w3)) @ w2

def _moe(h, router_w, router_b, w1, w3, w2):
    B, N, D = h.shape
    t = h.reshape(B * N, D)
    logits = (t @ router_w).astype(jnp.float32) + router_b.astype(jnp.float32)
    top_v, top_i = lax.top_k(logits, TOP_K)
    wts = jax.nn.softmax(top_v, axis=-1)
    gate = jnp.sum(jax.nn.one_hot(top_i, N_EXPERTS, dtype=jnp.float32) * wts[..., None], axis=1)
    gate = gate.astype(t.dtype)
    out = jnp.zeros_like(t)
    for e in range(N_EXPERTS):
        out = out + gate[:, e:e + 1] * _swiglu(t, w1[e], w3[e], w2[e])
    return out.reshape(B, N, D)

def _trunk(x, cond, rope, ctx_k, ctx_v, norm1_w, norm2_w, ada_w, ada_b, w_in, w_o,
           q_norm_w, k_norm_w, pool_w, pool_scale, ffn_w1, ffn_w3, ffn_w2,
           router_w, router_b, moe_w1, moe_w3, moe_w2):
    ks, vs = [], []
    s_cond = jax.nn.silu(cond)
    for l in range(DEPTH):
        mod = (s_cond @ ada_w[l] + ada_b[l])[:, None, :]
        sh1, sc1, g1, sh2, sc2, g2 = jnp.split(mod, 6, axis=-1)
        h = _rms_norm(x, norm1_w[l]) * (1 + sc1) + sh1
        kc = None if ctx_k is None else ctx_k[:, l]
        vc = None if ctx_v is None else ctx_v[:, l]
        mix_out, k, v = _mixer(h, w_in[l], w_o[l], q_norm_w[l], k_norm_w[l], pool_w[l],
                               pool_scale[l], rope, kc, vc)
        x = x + g1 * mix_out
        h = _rms_norm(x, norm2_w[l]) * (1 + sc2) + sh2
        if l % 2 == 0:
            f = _swiglu(h, ffn_w1[l // 2], ffn_w3[l // 2], ffn_w2[l // 2])
        else:
            f = _moe(h, router_w[l // 2], router_b[l // 2], moe_w1[l // 2], moe_w3[l // 2], moe_w2[l // 2])
        x = x + g2 * f
        ks.append(k)
        vs.append(v)
    return x, ks, vs

def setup_inputs(seed: int = 0) -> dict:
    key = jax.random.key(seed)
    ks = jax.random.split(key, 32)
    f32 = jnp.float32

    def nrm(k, shape, scale=1.0):
        return jax.random.normal(k, shape, f32) * scale

    D = D_MODEL
    return {
        "x_prompt": nrm(ks[0], (BATCH, SEQ, D)),
        "x_sample": nrm(ks[1], (DEC_BATCH, DEC_SEQ, D)),
        "cache_k": nrm(ks[2], (DEC_BATCH, DEPTH, PAST_LEN, N_KV_HEADS, HEAD_DIM)),
        "cache_v": nrm(ks[3], (DEC_BATCH, DEPTH, PAST_LEN, N_KV_HEADS, HEAD_DIM)),
        "c": nrm(ks[4], (DEC_BATCH, D)),
        "c_ctx": nrm(ks[5], (D,)),
        "norm1_w": 1.0 + nrm(ks[6], (DEPTH, D), 0.05),
        "norm2_w": 1.0 + nrm(ks[7], (DEPTH, D), 0.05),
        "ada_w": nrm(ks[8], (DEPTH, D, 6 * D), 0.5 * D ** -0.5),
        "ada_b": nrm(ks[9], (DEPTH, 6 * D), 0.02),
        "w_in": nrm(ks[10], (DEPTH, D, IN_COLS), D ** -0.5),
        "w_o": nrm(ks[11], (DEPTH, D_MIX, D), D_MIX ** -0.5),
        "q_norm_w": 1.0 + nrm(ks[12], (DEPTH, HEAD_DIM), 0.05),
        "k_norm_w": 1.0 + nrm(ks[13], (DEPTH, HEAD_DIM), 0.05),
        "pool_w": nrm(ks[14], (DEPTH, N_POOL_GROUPS, POOL_GC, POOL_GC), POOL_GC ** -0.5),
        "pool_scale": 1.0 + nrm(ks[15], (DEPTH, POOL_WIDTH), 0.1),
        "ffn_w1": nrm(ks[16], (N_DENSE, D, D_FF), D ** -0.5),
        "ffn_w3": nrm(ks[17], (N_DENSE, D, D_FF), D ** -0.5),
        "ffn_w2": nrm(ks[18], (N_DENSE, D_FF, D), D_FF ** -0.5),
        "router_w": nrm(ks[19], (N_MOE, D, N_EXPERTS), D ** -0.5),
        "router_b": nrm(ks[20], (N_MOE, N_EXPERTS), 0.01),
        "moe_w1": nrm(ks[21], (N_MOE, N_EXPERTS, D, D_FF_EXPERT), D ** -0.5),
        "moe_w3": nrm(ks[22], (N_MOE, N_EXPERTS, D, D_FF_EXPERT), D ** -0.5),
        "moe_w2": nrm(ks[23], (N_MOE, N_EXPERTS, D_FF_EXPERT, D), D_FF_EXPERT ** -0.5),
    }

def reference(x_prompt, x_sample, cache_k, cache_v, c, c_ctx, norm1_w, norm2_w, ada_w, ada_b,
              w_in, w_o, q_norm_w, k_norm_w, pool_w, pool_scale, ffn_w1, ffn_w3, ffn_w2,
              router_w, router_b, moe_w1, moe_w3, moe_w2):
    y_prompt, kp, vp = _trunk(x_prompt, c_ctx[None, :], None, None, None,
                              norm1_w, norm2_w, ada_w, ada_b, w_in, w_o, q_norm_w, k_norm_w,
                              pool_w, pool_scale, ffn_w1, ffn_w3, ffn_w2,
                              router_w, router_b, moe_w1, moe_w3, moe_w2)
    new_k = jnp.stack(kp, axis=1)
    new_v = jnp.stack(vp, axis=1)
    rope = _axial_rope(x_sample.shape[1])
    y_sample, _, _ = _trunk(x_sample, c, rope, cache_k, cache_v,
                            norm1_w, norm2_w, ada_w, ada_b, w_in, w_o, q_norm_w, k_norm_w,
                            pool_w, pool_scale, ffn_w1, ffn_w3, ffn_w2,
                            router_w, router_b, moe_w1, moe_w3, moe_w2)
    return (y_prompt, y_sample, new_k, new_v)


_drawn_inputs = setup_inputs


def setup_inputs(seed=0):
    import zlib

    import numpy as np

    out = dict(_drawn_inputs(seed))
    spreads = {}
    factors = {'cache_k': 3.165, 'cache_v': 3.021, 'q_norm_w': 8.0, 'router_b': 22.444}
    for name, (base, spread) in spreads.items():
        noise = np.random.default_rng([zlib.crc32(name.encode()), seed]).standard_normal(out[name].shape)
        drawn = base * np.exp(spread * noise) if base else spread * noise
        out[name] = __import__('jax').numpy.asarray(drawn.astype(out[name].dtype))
    for name, factor in factors.items():
        out[name] = (out[name] * factor).astype(out[name].dtype)
    return out
```

```python
import concourse.bass as bass
from concourse import mybir
from contextlib import ExitStack
import numpy as np

P = 128
D = 1024
KD = D // P
DEPTH = 2
N_PROMPT, N_SAMPLE, PAST = 128, 256, 128
N = N_PROMPT + N_SAMPLE
NT = N // P
HD = 64
N_HEADS, N_KV = 8, 2
ATTN = N_HEADS * HD
KV_W = N_KV * HD
POOL_W = D - ATTN
WINDOWS = (2, 4, 8, 16)
NG = len(WINDOWS)
IN_COLS = ATTN + 2 * KV_W + POOL_W
FF = 2816
NF = FF // P
NE = 8
GRID_W = 64
THETA = 10000.0
EPS = 1e-6
SLOTS = 11
UCOLS = 256
UNIT = KD * UCOLS
MODS = 6 * KD
ADA_UNITS = 6 * D // UCOLS
MIX_UNITS = 6 + D // UCOLS
FF_UNITS = 3 * NF // 2
NQ = ATTN // P
NQK = NQ + N_KV
PAD = max(WINDOWS) // 2
PADW = PAD + N_PROMPT + PAD + N_SAMPLE + PAD
SEQS = ((0, N_PROMPT), (N_PROMPT, N))
PADDED = (PAD, 2 * PAD + N_PROMPT)
WIDTHS = (128, 192, 384)
UNITS = [(t, h) for t in range(NT) for h in range(N_HEADS)]
NU = len(UNITS)

C_ID, C_ONE, C_BLK, C_PERM, C_TRI = 0, P, 2 * P, 3 * P, 4 * P
C_IOTA = 5 * P
C_RANK = C_IOTA + N
N_CONST = C_RANK + NE
M_COS, M_SIN, M_INV = 0, N_SAMPLE, 2 * N_SAMPLE
N_MTAB = M_INV + NG * N


def constants():
    c = np.zeros((P, N_CONST), np.float32)
    i = np.arange(P)
    c[:, C_ID:C_ID + P] = np.eye(P)
    c[:, C_ONE:C_ONE + P] = 1.0
    c[:, C_BLK:C_BLK + P] = (i[:, None] // HD == i[None, :] // HD)
    nf = HD // 4
    half = (i // nf) % 2
    partner = np.where(half == 0, i + nf, i - nf)
    c[partner, C_PERM + i] = np.where(half == 0, -1.0, 1.0)
    c[:, C_TRI:C_TRI + P] = (i[:, None] < i[None, :])
    c[:, C_IOTA:C_IOTA + N] = np.arange(N)[None, :]
    c[:, C_RANK:C_RANK + NE] = (NE - np.arange(NE))[None, :]
    m = np.zeros((P, N_MTAB), np.float32)
    inv = (np.float32(THETA) ** (-np.arange(nf, dtype=np.float32) / np.float32(nf))).astype(np.float32)
    t = np.arange(N_SAMPLE)
    pos = np.stack([(t // GRID_W), (t % GRID_W)]).astype(np.float32)
    ang = pos[(i % HD) // (2 * nf)] * inv[i % nf][:, None]
    m[:, M_COS:M_COS + N_SAMPLE] = np.cos(ang)
    m[:, M_SIN:M_SIN + N_SAMPLE] = np.sin(ang)
    for g, w in enumerate(WINDOWS):
        for a, b in SEQS:
            n = b - a
            k = np.arange(n)
            cnt = np.clip(k + w // 2, 0, n) - np.clip(k - w // 2, 0, n)
            m[:, M_INV + g * N + a:M_INV + g * N + b] = (1.0 / cnt.astype(np.float32))[None, :]
    return c, m


def build(nc, x_prompt, x_sample, cache_k, cache_v, c, c_ctx, norm1_w, norm2_w, ada_w, ada_b,
          w_in, w_o, q_norm_w, k_norm_w, pool_w, pool_scale, ffn_w1, ffn_w3, ffn_w2,
          router_w, router_b, moe_w1, moe_w3, moe_w2, const_tab, mix_tab,
          y_prompt, y_sample, new_k, new_v):
    f32 = mybir.dt.float32
    i32 = mybir.dt.int32
    ALU = mybir.AluOpType
    ACT = mybir.ActivationFunctionType
    AX = mybir.AxisListType
    ds = bass.ds

    ctx = ExitStack()
    with ctx:
        def sb(name, shape, dt=f32):
            return ctx.enter_context(nc.sbuf_tensor(name, shape, dt))

        def sem(name):
            return ctx.enter_context(nc.semaphore(name))

        ring = sb("ring", [P, SLOTS, UNIT])
        xT = sb("xT", [P, KD, N])
        hT = sb("hT", [P, KD, N])
        arena = sb("arena", [P, NF * N + 3 * KD * N])
        shared = sb("shared", [P, 3 * NT * N])
        silu_h = sb("silu_h", [P, 2, N])
        const = sb("const", [P, N_CONST])
        cols = sb("cols", [P, 2, P])
        condT = sb("condT", [P, KD, 2])
        mod = sb("mod", [P, DEPTH, MODS, 2])
        scale_n = sb("scale_n", [P, 2 * DEPTH, KD, 2])
        rstd = sb("rstd", [P, N])
        att = sb("att", [P, 3, 4])
        rsmall = sb("rsmall", [P, 8, NT])
        rw = sb("rw", [P, KD, NE])
        rb = sb("rb", [1, NE])
        route = sb("route", [P, NE, 2, NT])
        cur = sb("cur", [P, 2 * NT])
        counts = sb("counts", [1, NE], i32)

        def part(t, at, *dims):
            n = int(np.prod(dims))
            v = t[:, at:at + n]
            if len(dims) == 2:
                return v.rearrange("p (a b) -> p a b", a=dims[0])
            if len(dims) == 3:
                return v.rearrange("p (a b c) -> p a b c", a=dims[0], b=dims[1])
            return v

        small = silu_h[:].rearrange("p a n -> p (a n)")
        rows = part(small, 0, 2, P)
        rt = part(small, 2 * P, 11, NT, NE)
        x_nat = part(arena, 0, NT, D)
        qn = part(arena, 0, NQK, N)
        raw = part(arena, NQK * N, NQK, N)
        sq = part(arena, 2 * NQK * N, NQK, N)
        hr = part(arena, 3 * NQK * N, NQK, N)
        v_new = part(arena, 9216, NT, KV_W)
        mixT = part(arena, 9600, KD, N)
        upad = part(arena, 12672, NG, PADW)
        psum_w = part(arena, 14304, 2, PADW)
        rope_a = part(arena, 15120, 2, N_SAMPLE)
        rope_b = part(arena, 15632, 2, N_SAMPLE)
        k_nat = part(arena, 16144, N_KV, P)
        kc_nat = part(arena, 16400, DEPTH, N_KV * P)
        vc = part(arena, 16912, DEPTH, KV_W)
        kcT = part(arena, 17168, N_KV, PAST)
        probs, probsT = raw, sq
        gT = part(arena, 0, NF, N)
        y_sb = part(arena, NF * N, NT, D)
        h_nat = part(arena, NF * N + KD * N, NT, D)
        heT = part(arena, NF * N + 2 * KD * N, KD, N)
        mtab = part(shared, 0, N_MTAB)
        pw = part(shared, N_MTAB, DEPTH * NG, P)
        onehot = part(shared, 0, NT, N)
        gated = part(shared, NT * N, NT, N)
        gatedT = part(shared, 2 * NT * N, NT, N)
        assert N_MTAB + DEPTH * NG * P <= 3 * NT * N

        bank = [ctx.enter_context(nc.psum_tensor(f"bank{i}", [P, 512], f32)) for i in range(8)]
        ident = const[:, C_ID:C_ID + P]
        ones = const[:, C_ONE:C_ONE + P]
        blocks = const[:, C_BLK:C_BLK + P]
        perm = const[:, C_PERM:C_PERM + P]
        tri = const[:, C_TRI:C_TRI + P]
        iota = const[:, C_IOTA:C_IOTA + N]
        rank = const[:, C_RANK:C_RANK + NE]
        R_CTX, R_C, R_PS, R_QN, R_KN, R_END = 0, KD, 2 * KD, 2 * KD + DEPTH * NG, 2 * KD + DEPTH * NG + 2, 2 * KD + DEPTH * NG + 4

        def adab(l):
            return cols[:, 0, l * MODS:(l + 1) * MODS]

        def normw(n):
            a = DEPTH * MODS + (n % 2) * DEPTH * KD + (n // 2) * KD
            return cols[:, 0, a:a + KD]

        slot_full = [sem(f"slot_full{s}") for s in range(SLOTS)]
        A0 = [0, ADA_UNITS + MIX_UNITS + FF_UNITS]
        M0 = [a + ADA_UNITS for a in A0]
        F0 = [m + MIX_UNITS for m in M0]

        def slot(i):
            return ring[:, i % SLOTS, :]

        def block(i):
            return slot(i).rearrange("p (k n) -> p k n", k=KD)

        def loads(i):
            return i // SLOTS + 1 + 3 * sum(m + 2 <= i and (i - m - 2) % SLOTS == 0 for m in M0)

        def wait_unit(eng, i, e=0):
            eng.wait_ge(slot_full[i % SLOTS], e * (16 * FF_UNITS // SLOTS) + 16 * loads(i))

        s_x, s_const, s_mtab, s_rows, s_pw, s_cache, s_router = map(
            sem, ("x_in", "const_in", "mtab_in", "rows_in", "pw_in", "cache_in", "router_in"))
        s_xt, s_xa, s_xv = sem("x_transposed"), sem("x_kept_act"), sem("x_kept_dve")
        s_colsT, s_cols, s_cond = sem("cols_transposed"), sem("cols_kept"), sem("cond_silu")
        s_pad = sem("pads_zeroed")
        s_dve, s_act, s_pool = sem("dve_step"), sem("act_step"), sem("pool_step")
        per = lambda name, n=DEPTH: [sem(f"{name}{i}") for i in range(n)]
        s_ada, s_mod = per("ada_done"), per("mod_ready")
        s_nsq, s_nss, s_nvar, s_nstd, s_nt, s_nh = (per(n, 2 * DEPTH) for n in (
            "norm_squares", "norm_sum", "norm_var", "norm_std", "norm_scaled", "norm_out"))
        s_proj, s_raw, s_sq, s_ss = per("proj_done"), per("raw_kept"), per("squares"), per("head_sum")
        s_var, s_std, s_qn, s_rot, s_ra, s_qk = (per(n) for n in (
            "head_var", "head_std", "head_normed", "rotated", "rope_cos", "qk_ready"))
        s_u, s_v, s_kt, s_kn = per("u_kept"), per("v_kept"), per("k_transposed"), per("k_nat_kept")
        s_kct, s_kck = per("cache_transposed"), per("cache_kept")
        s_d, s_pool_mm, s_pooled = per("pool_diff"), per("pool_product"), per("pooled")
        s_sc, s_mx, s_ex, s_pn, s_pt, s_ptk, s_pv, s_av = (per(n) for n in (
            "scores", "score_max", "probs_exp", "probs_normed", "probs_transposed", "probsT_kept",
            "pv_done", "attn_kept"))
        s_wo, s_x1, s_vp = per("wo_done"), per("x_after_mixer"), per("v_done")
        s_out, s_kv = sem("stores"), per("kv_stores")
        ff_names = ("h1", "h3", "silu", "g", "down", "y_act", "y_dve", "back", "x_add")
        FFN = {n: sem(f"ffn_{n}") for n in ff_names}
        MOE = {n: sem(f"moe_{n}") for n in ff_names if n != "x_add"}
        s_xadd = MOE["x_add"] = FFN["x_add"]
        s_hnt, s_hna, s_hnv = sem("h_nat_transposed"), sem("h_nat_act"), sem("h_nat_dve")
        s_lg, s_dl, s_ed, s_sel, s_posd, s_route = map(sem, (
            "logits", "top2_gap", "top2_exp", "selected", "positions", "routed"))
        s_cur, s_oh, s_gd, s_ga, s_gv, s_gt, s_gtk = map(sem, (
            "cur_copied", "onehot_ready", "gathered", "gathered_act", "gathered_dve",
            "gate_transposed", "gateT_kept"))
        s_yt, s_ya, s_yv = sem("y_transposed"), sem("y_kept_act"), sem("y_kept_dve")

        N_ROW_LOADS, N_CACHE_LOADS = 10, 3 * DEPTH

        def by_count(eng, e, body):
            n = eng.value_load(counts[:, ds(e, 1)], min_val=0, max_val=N)
            with eng.If(n <= WIDTHS[0]):
                body(WIDTHS[0])
            with eng.Else():
                with eng.If(n <= WIDTHS[1]):
                    body(WIDTHS[1])
                with eng.Else():
                    body(WIDTHS[2])

        blockctx = ctx.enter_context(nc.Block())

        @blockctx.sync
        def _(sp):
            def used(i):
                for l in range(DEPTH):
                    if i < M0[l]:
                        return s_ada[l], i - A0[l] + 1
                    if i < M0[l] + 5:
                        return s_proj[l], 2 * (i - M0[l]) + 2
                    if i == M0[l] + 5:
                        return s_vp[l], 1
                    if i < F0[l]:
                        return s_wo[l], 2 * (i - M0[l] - 6) + 2
                    if i < F0[l] + FF_UNITS:
                        return used_ff(FFN, i - F0[l])

            def used_ff(S, j):
                if j < NF:
                    return S[("h1", "h3")[j % 2]], j // 2 * 2 + 2
                return S["down"], j - NF + 1

            def free(i):
                if i >= SLOTS:
                    sp.wait_ge(*used(i - SLOTS))

            def columns(i, w, a, n=UCOLS):
                free(i)
                sp.dma_start(block(i)[:, :, 0:n],
                             w[:, a:a + n].rearrange("(k p) n -> p k n", p=P)).then_inc(slot_full[i % SLOTS], 16)

            for l in range(DEPTH):
                for u in range(ADA_UNITS):
                    columns(A0[l] + u, ada_w[l], u * UCOLS)
                m = M0[l]
                columns(m, w_in[l], 0)
                columns(m + 1, w_in[l], UCOLS)
                free(m + 2)
                dst = block(m + 2).rearrange("p k (g r n) -> p k g r n", g=N_KV, r=2)
                for g in range(N_KV):
                    src = w_in[l][:, ATTN + g * HD:ATTN + (g + 1) * HD].rearrange("(k p) n -> p k n", p=P)
                    for r in range(2):
                        sp.dma_start(dst[:, :, g, r, :], src).then_inc(slot_full[(m + 2) % SLOTS], 16)
                columns(m + 3, w_in[l], ATTN + 2 * KV_W)
                columns(m + 4, w_in[l], ATTN + 2 * KV_W + UCOLS)
                columns(m + 5, w_in[l], ATTN + KV_W, KV_W)
                for u in range(D // UCOLS):
                    columns(m + 6 + u, w_o[l], u * UCOLS)
                if l == 0:
                    for u in range(NF // 2):
                        columns(F0[0] + 2 * u, ffn_w1[0], u * UCOLS)
                        columns(F0[0] + 2 * u + 1, ffn_w3[0], u * UCOLS)
                    for u in range(NF // 2):
                        free(F0[0] + NF + u)
                        sp.dma_start(slot(F0[0] + NF + u).rearrange("p (f n) -> p f n", f=2),
                                     ffn_w2[0][u * 2 * P:(u + 1) * 2 * P, :].rearrange("(f p) n -> p f n", p=P)
                                     ).then_inc(slot_full[(F0[0] + NF + u) % SLOTS], 16)

            def expert_unit(j, e):
                i = F0[1] + j
                if j < NF:
                    w = (moe_w1, moe_w3)[j % 2][0, ds(e, 1)].rearrange("o k n -> (o k) n")
                    a = j // 2 * UCOLS
                    sp.dma_start(block(i), w[:, a:a + UCOLS].rearrange("(k p) n -> p k n", p=P)
                                 ).then_inc(slot_full[i % SLOTS], 16)
                else:
                    w = moe_w2[0, ds(e, 1)].rearrange("o k n -> (o k) n")
                    a = (j - NF) * 2 * P
                    sp.dma_start(slot(i).rearrange("p (f n) -> p f n", f=2),
                                 w[a:a + 2 * P, :].rearrange("(f p) n -> p f n", p=P)
                                 ).then_inc(slot_full[i % SLOTS], 16)

            def rest_of_expert(e):
                for j in range(SLOTS, FF_UNITS):
                    s, v = used_ff(MOE, j - SLOTS)
                    if j != NF:
                        sp.wait_ge(s, e * NF + v)
                    if j == NF - 1:
                        s, v = used_ff(MOE, NF - SLOTS)
                        sp.wait_ge(s, e * NF + v)
                    expert_unit(j, e)

            for j in range(SLOTS):
                free(F0[1] + j)
                expert_unit(j, 0)
            with sp.Fori(0, NE - 1) as e:
                rest_of_expert(e)
                for j in range(SLOTS):
                    sp.wait_ge(MOE["down"], e * (NF // 2) + j + 1)
                    expert_unit(j, e + 1)
            rest_of_expert(NE - 1)
            sp.wait_ge(s_ya, NT)
            sp.wait_ge(s_yv, NT)
            sp.dma_start(y_prompt[0], y_sb[:, 0, :]).then_inc(s_out, 16)
            sp.dma_start(y_sample[0].rearrange("(t p) d -> p t d", p=P), y_sb[:, 1:NT, :]).then_inc(s_out, 16)
            sp.wait_ge(s_out, 32)
            for l in range(DEPTH):
                sp.wait_ge(s_kv[l], 32)

        @blockctx.tensor
        def _(pe):
            mm, tr = nc.tensor.matmul, nc.tensor.transpose

            pe.wait_ge(s_const, 16)
            pe.wait_ge(s_x, 32)
            for k in range(KD):
                for t in range(NT):
                    last = tr(bank[k][:, t * P:(t + 1) * P], x_nat[:, t, k * P:(k + 1) * P], ident)
                last.then_inc(s_xt, 1)
            pe.wait_ge(s_rows, 16 * N_ROW_LOADS)
            pe.wait_ge(s_xa, 1)
            tr(bank[0][:, 0:P], rows[:, 0, :], ident)
            pe.wait_ge(s_xv, 1)
            tr(bank[1][:, 0:R_END], rows[0:R_END, 1, :], ident[0:R_END, 0:R_END]).then_inc(s_colsT, 1)

            def ada(l):
                if l == 0:
                    pe.wait_ge(s_cond, 1)
                    pe.wait_ge(s_xv, 2)
                for u in range(ADA_UNITS):
                    wait_unit(pe, A0[l] + u)
                    w = block(A0[l] + u)
                    for c2 in range(2):
                        at = 2 * (2 * u + c2)
                        for k in range(KD):
                            last = mm(bank[3][:, at:at + 2], w[:, k, c2 * P:(c2 + 1) * P], condT[:, k, :],
                                      start=(k == 0), stop=(k == KD - 1))
                    last.then_inc(s_ada[l], 1)

            def norm(n):
                for k in range(KD):
                    pe.wait_ge(s_nsq[n], k + 1)
                    last = mm(bank[0][:, 0:N], ones, hT[:, k, :], start=(k == 0), stop=(k == KD - 1))
                last.then_inc(s_nss[n], 1)

            def projections(l):
                m = M0[l]
                nchunk = NQK + NG
                for j in range(nchunk + 3):
                    if j < nchunk:
                        if j % 2 == 0:
                            wait_unit(pe, m + j // 2)
                        w = block(m + j // 2)
                        if 3 <= j < NQK + 3:
                            pe.wait_ge(s_sq[l], j - 2)
                        elif j >= NQK + 3:
                            pe.wait_ge(s_u[l], j - 2 - NQK)
                        for k in range(KD):
                            if j == 0:
                                pe.wait_ge(s_nh[2 * l], k + 1)
                            last = mm(bank[j % 3][:, 0:N], w[:, k, (j % 2) * P:(j % 2 + 1) * P], hT[:, k, :],
                                      start=(k == 0), stop=(k == KD - 1))
                        last.then_inc(s_proj[l], 1)
                    i = j - 1
                    if 0 <= i < NQK:
                        pe.wait_ge(s_sq[l], i + 1)
                        if i >= 2:
                            pe.wait_ge(s_var[l], i - 1)
                        mm(bank[3 + i % 2][:, 0:N], blocks, sq[:, i, :], start=True, stop=True).then_inc(s_ss[l], 1)
                    i = j - 3
                    if 0 <= i < NQK:
                        pe.wait_ge(s_qn[l], i + 1)
                        if i >= 2:
                            pe.wait_ge(s_qk[l], i - 1)
                        mm(bank[5 + i % 2][:, 0:N_SAMPLE], perm, qn[:, i, N_PROMPT:N],
                           start=True, stop=True).then_inc(s_rot[l], 1)
                wait_unit(pe, m + 5)
                w = block(m + 5)
                pe.wait_ge(s_u[l], NG)
                for t in range(NT):
                    for k in range(KD):
                        last = mm(bank[0][:, t * KV_W:(t + 1) * KV_W], hT[:, k, t * P:(t + 1) * P],
                                  w[:, k, 0:KV_W], start=(k == 0), stop=(k == KD - 1))
                last.then_inc(s_vp[l], 1)
                pe.wait_ge(s_var[l], NQK)
                for g in range(N_KV):
                    last = tr(bank[3][:, g * P:(g + 1) * P], qn[:, NQ + g, 0:N_PROMPT], ident)
                last.then_inc(s_kt[l], 1)
                pe.wait_ge(s_cache, 16 * N_CACHE_LOADS)
                for g in range(N_KV):
                    last = tr(bank[4][:, g * P:(g + 1) * P], kc_nat[:, l, g * P:(g + 1) * P], ident)
                last.then_inc(s_kct[l], 1)

            def pooling(l):
                pe.wait_ge(s_pw, 16)
                for g in range(NG):
                    pe.wait_ge(s_d[l], g + 1)
                    if g == 0:
                        pe.wait_ge(s_av[l], NU // 2)
                    if g >= 2:
                        pe.wait_ge(s_pooled[l], g - 1)
                    mm(bank[g % 2][:, 0:N], pw[:, l * NG + g, :], mixT[:, NQ + g, :],
                       start=True, stop=True).then_inc(s_pool_mm[l], 1)

            def attention(l):
                pe.wait_ge(s_qk[l], NQK)
                pe.wait_ge(s_kck[l], 1)
                pe.wait_ge(s_v[l], 1)
                pe.wait_ge(s_kn[l], 1)
                for s in range(NU + 3):
                    if s < NU:
                        t, h = UNITS[s]
                        g, a = h // (N_HEADS // N_KV), h % 2 * HD
                        if s >= 3:
                            pe.wait_ge(s_ex[l], s - 2)
                        b = bank[s % 3]
                        q = qn[a:a + HD, h // 2, t * P:(t + 1) * P]
                        k = qn[a:a + HD, NQ + g, :]
                        if t == 0:
                            last = mm(b[:, 0:N_PROMPT], q, k[:, 0:N_PROMPT], start=True, stop=True)
                        else:
                            mm(b[:, 0:N_SAMPLE], q, k[:, N_PROMPT:N], start=True, stop=True)
                            last = mm(b[:, N_SAMPLE:N_SAMPLE + PAST], q, kcT[a:a + HD, g, :], start=True, stop=True)
                        last.then_inc(s_sc[l], 1)
                    i = s - 2
                    if 0 <= i < NU:
                        t, h = UNITS[i]
                        pe.wait_ge(s_pn[l], i + 1)
                        if i >= 2:
                            pe.wait_ge(s_ptk[l], i - 1)
                        for kt in range(1 if t == 0 else NT):
                            last = tr(bank[3 + i % 2][:, kt * P:(kt + 1) * P],
                                      probs[:, i % 3, kt * P:(kt + 1) * P], ident)
                        last.then_inc(s_pt[l], 1)
                    i = s - 3
                    if 0 <= i < NU:
                        t, h = UNITS[i]
                        g, a = h // (N_HEADS // N_KV), h % 2 * HD
                        pe.wait_ge(s_ptk[l], i + 1)
                        if i >= 4 and i % 2 == 0:
                            pe.wait_ge(s_av[l], i // 2 - 1)
                        b = bank[5 + i // 2 % 2]
                        vs = [v_new[:, 0, :]] if t == 0 else [v_new[:, 1, :], v_new[:, 2, :], vc[:, l, :]]
                        for kt, v in enumerate(vs):
                            last = mm(b[a:a + HD, 0:P], v[:, g * HD:(g + 1) * HD],
                                      probsT[:, i % 2, kt * P:(kt + 1) * P],
                                      start=(kt == 0), stop=(kt == len(vs) - 1))
                        last.then_inc(s_pv[l], 1)

            def output(l):
                pe.wait_ge(s_pooled[l], NG)
                for d in range(KD):
                    i = M0[l] + 6 + d // 2
                    if d % 2 == 0:
                        wait_unit(pe, i)
                    if d >= 4:
                        pe.wait_ge(s_x1[l], d - 3)
                    for k in range(KD):
                        last = mm(bank[2 + d % 4][:, 0:N], block(i)[:, k, d % 2 * P:(d % 2 + 1) * P], mixT[:, k, :],
                                  start=(k == 0), stop=(k == KD - 1))
                    last.then_inc(s_wo[l], 1)

            def up(S, F, e, src, w):
                for f in range(NF):
                    for which, name, reader in ((0, "h1", "silu"), (1, "h3", "g")):
                        i = F + f // 2 * 2 + which
                        b = bank[f % 2 * 2 + which]
                        if f % 2 == 0:
                            wait_unit(pe, i, e)
                        if f >= 2:
                            pe.wait_ge(S[reader], e * NF + f - 1)
                        for k in range(KD):
                            last = mm(b[:, 0:w], block(i)[:, k, f % 2 * P:(f % 2 + 1) * P], src[:, k, 0:w],
                                      start=(k == 0), stop=(k == KD - 1))
                        last.then_inc(S[name], 1)

            def down(S, F, e, w):
                if w > 2 * P:
                    pe.wait_ge(S["g"], e * NF + NF)
                for f in range(NF):
                    i = F + NF + f // 2
                    if f % 2 == 0:
                        wait_unit(pe, i, e)
                    pe.wait_ge(S["g"], e * NF + f + 1)
                    w2 = slot(i).rearrange("p (f n) -> p f n", f=2)[:, f % 2, :]
                    for s in range(0, w, P):
                        m = min(P, w - s)
                        for half in range(2):
                            last = mm(bank[6 - s // P * 2 + half][0:m, :], gT[:, f, s:s + m],
                                      w2[:, half * 512:(half + 1) * 512], start=(f == 0), stop=(f == NF - 1))
                    if f % 2 == 1:
                        last.then_inc(S["down"], 1)

            def dense():
                up(FFN, F0[0], 0, hT, N)
                down(FFN, F0[0], 0, N)
                pe.wait_ge(FFN["y_act"], 1)
                pe.wait_ge(FFN["y_dve"], 1)
                for d in range(KD):
                    if d >= 4:
                        pe.wait_ge(FFN["x_add"], d - 3)
                    for t in range(NT):
                        last = tr(bank[4 + d % 4][:, t * P:(t + 1) * P], y_sb[:, t, d * P:(d + 1) * P], ident)
                    last.then_inc(FFN["back"], 1)

            def routing():
                pe.wait_ge(s_nh[3], KD)
                pe.wait_ge(s_router, 32)
                for t in range(NT):
                    b = bank[4][:, t * NE:(t + 1) * NE]
                    for k in range(KD):
                        mm(b, hT[:, k, t * P:(t + 1) * P], rw[:, k, :], start=(k == 0), stop=False)
                    last = mm(b, ones[0:1, :], rb[0:1, :], start=False, stop=True)
                last.then_inc(s_lg, 1)
                for t in range(NT):
                    for i in range(2):
                        if t == 2:
                            pe.wait_ge((s_hna, s_hnv)[i], 1)
                        for k in range(4):
                            d = 4 * i + k
                            last = tr(bank[2 * (t % 2) + i][:, k * P:(k + 1) * P], hT[:, d, t * P:(t + 1) * P], ident)
                        last.then_inc(s_hnt, 1)
                pe.wait_ge(s_sel, 1)
                sel = rt[:, 10, :, :]
                for t in range(NT):
                    b = bank[5][:, t * NE:(t + 1) * NE]
                    mm(b, tri, sel[:, t, :], start=True, stop=(t == 0))
                    for s in range(t):
                        mm(b, ones, sel[:, s, :], start=False, stop=(s == t - 1))
                for t in range(NT):
                    last = mm(bank[6][:, 0:NE], ones, sel[:, t, :], start=(t == 0), stop=(t == NT - 1))
                last.then_inc(s_posd, 1)

            def gather(e, w):
                pe.wait_ge(s_oh, e * 2 + 1)
                for k in range(KD):
                    if k >= 4:
                        pe.wait_ge((s_ga, s_gv)[k % 2], e * (KD // 2) + k // 2 - 1)
                    for t in range(NT):
                        last = mm(bank[k % 4][:, 0:w], h_nat[:, t, k * P:(k + 1) * P], onehot[:, t, 0:w],
                                  start=(t == 0), stop=(t == NT - 1))
                    last.then_inc(s_gd, 1)
                pe.wait_ge(s_oh, e * 2 + 2)
                for s in range(0, w, P):
                    m = min(P, w - s)
                    for t in range(NT):
                        last = tr(bank[4 + s // P][0:m, t * P:(t + 1) * P], gated[:, t, s:s + m], ident)
                last.then_inc(s_gt, 1)
                pe.wait_ge(s_ga, e * (KD // 2) + KD // 2)
                pe.wait_ge(s_gv, e * (KD // 2) + KD // 2)

            def scatter(e, w):
                pe.wait_ge(MOE["y_act"], e + 1)
                pe.wait_ge(MOE["y_dve"], e + 1)
                pe.wait_ge(s_gtk, e + 1)
                for d in range(KD):
                    if d >= 4:
                        pe.wait_ge(s_xadd, e * KD + KD + d - 3)
                    for s in range(0, w, P):
                        m = min(P, w - s)
                        last = mm(bank[4 + d % 4][:, 0:N], y_sb[0:m, s // P, d * P:(d + 1) * P],
                                  gatedT[0:m, s // P, :], start=(s == 0), stop=(s + P >= w))
                    last.then_inc(MOE["back"], 1)

            for l in range(DEPTH):
                ada(l)
                norm(2 * l)
                projections(l)
                attention(l)
                pooling(l)
                output(l)
                norm(2 * l + 1)
                if l == 0:
                    for k in range(KD):
                        pe.wait_ge(s_nh[1], k + 1)
                    dense()
            routing()
            pe.wait_ge(s_route, 1)
            pe.wait_ge(s_hna, NT)
            pe.wait_ge(s_hnv, NT)

            def expert(e, w):
                gather(e, w)
                up(MOE, F0[1], e, heT, w)
                down(MOE, F0[1], e, w)
                scatter(e, w)

            with pe.Fori(0, NE) as e:
                by_count(pe, e, lambda w: expert(e, w))
            pe.wait_ge(s_xadd, NE * KD + KD)
            for t in range(NT):
                for i in range(2):
                    for k in range(4):
                        last = tr(bank[2 * t + i][:, k * P:(k + 1) * P], xT[:, 4 * i + k, t * P:(t + 1) * P], ident)
                    last.then_inc(s_yt, 1)

        @blockctx.scalar
        def _(act):
            A = nc.scalar.activation
            steps = [0]

            def step(ins):
                steps[0] += 1
                ins.then_inc(s_act, 1)
                act.wait_ge(s_act, steps[0])

            act.dma_start(x_nat[:, 0, :], x_prompt[0]).then_inc(s_x, 16)
            act.dma_start(x_nat[:, 1:NT, :], x_sample[0].rearrange("(t p) d -> p t d", p=P)).then_inc(s_x, 16)
            act.dma_start(const[:], const_tab).then_inc(s_const, 16)
            n_mod = DEPTH * MODS
            for dst, src in (
                    (rows[0:n_mod, 0, :], ada_b.rearrange("l (r c) -> (l r) c", c=P)),
                    (rows[n_mod:n_mod + DEPTH * KD, 0, :], norm1_w.rearrange("l (r c) -> (l r) c", c=P)),
                    (rows[n_mod + DEPTH * KD:P, 0, :], norm2_w.rearrange("l (r c) -> (l r) c", c=P)),
                    (rows[R_CTX:R_CTX + KD, 1, :], c_ctx.rearrange("(r c) -> r c", c=P)),
                    (rows[R_C:R_C + KD, 1, :], c[0].rearrange("(r c) -> r c", c=P)),
                    (rows[R_PS:R_QN, 1, :], pool_scale.rearrange("l (r c) -> (l r) c", c=P)),
                    (rows[R_QN:R_KN, 1, 0:HD], q_norm_w), (rows[R_QN:R_KN, 1, HD:P], q_norm_w),
                    (rows[R_KN:R_END, 1, 0:HD], k_norm_w), (rows[R_KN:R_END, 1, HD:P], k_norm_w)):
                act.dma_start(dst, src).then_inc(s_rows, 16)
            act.dma_start(mtab, mix_tab).then_inc(s_mtab, 16)
            act.dma_start(pw, pool_w.rearrange("l g c d -> c (l g) d")).then_inc(s_pw, 16)
            kcv = kc_nat.rearrange("p l (g r n) -> p l g r n", g=N_KV, r=2)
            for l in range(DEPTH):
                for r in range(2):
                    act.dma_start(kcv[:, l, :, r, :], cache_k[0, l]).then_inc(s_cache, 16)
                act.dma_start(vc[:, l, :], cache_v[0, l].rearrange("s g n -> s (g n)")).then_inc(s_cache, 16)
            act.dma_start(rw[:], router_w[0].rearrange("(k p) n -> p k n", p=P)).then_inc(s_router, 16)
            act.dma_start(rb[:], router_b).then_inc(s_router, 16)

            for k in range(0, KD, 2):
                act.wait_ge(s_xt, k + 1)
                A(xT[:, k, :], bank[k][:, 0:N], ACT.Copy).then_inc(s_xa, 1)
            act.wait_ge(s_cols, 2)
            A(condT[:, :, 0], cols[:, 1, R_CTX:R_CTX + KD], ACT.Silu)
            A(condT[:, :, 1], cols[:, 1, R_C:R_C + KD], ACT.Silu).then_inc(s_cond, 1)

            def norm(n):
                for k in range(KD):
                    if n == 0:
                        if k == 0:
                            act.wait_ge(s_xa, KD // 2)
                            act.wait_ge(s_xv, KD // 2)
                    elif n % 2 == 1:
                        act.wait_ge(s_x1[n // 2], k + 1)
                    else:
                        act.wait_ge(FFN["x_add"], k + 1)
                    A(hT[:, k, :], xT[:, k, :], ACT.Square).then_inc(s_nsq[n], 1)
                act.wait_ge(s_nvar[n], 1)
                A(rstd[:], rstd[:], ACT.Sqrt).then_inc(s_nstd[n], 1)
                sh = 0 if n % 2 == 0 else 3 * KD
                for k in range(KD):
                    act.wait_ge(s_nt[n], k + 1)
                    for q, (a, b) in enumerate(SEQS):
                        last = A(hT[:, k, a:b], hT[:, k, a:b], ACT.Identity,
                                 bias=mod[:, n // 2, sh + k, q:q + 1], scale=scale_n[:, n, k, q:q + 1])
                    last.then_inc(s_nh[n], 1)

            def projections(l):
                for j in range(NQK + 1):
                    if j < NQK:
                        act.wait_ge(s_proj[l], j + 1)
                        A(raw[:, j, :], bank[j % 3][:, 0:N], ACT.Copy).then_inc(s_raw[l], 1)
                        A(sq[:, j, :], bank[j % 3][:, 0:N], ACT.Square).then_inc(s_sq[l], 1)
                    if j >= 1:
                        act.wait_ge(s_var[l], j)
                        A(hr[:, j - 1, :], hr[:, j - 1, :], ACT.Sqrt).then_inc(s_std[l], 1)
                act.wait_ge(s_pad, 1)
                for g in range(NG):
                    act.wait_ge(s_proj[l], NQK + g + 1)
                    for (a, b), at in zip(SEQS, PADDED):
                        last = A(upad[:, g, at:at + b - a], bank[(NQK + g) % 3][:, a:b], ACT.Copy)
                    last.then_inc(s_u[l], 1)
                act.wait_ge(s_vp[l], 1)
                A(v_new[:], bank[0][:, 0:NT * KV_W].rearrange("p (t n) -> p t n", t=NT), ACT.Copy).then_inc(s_v[l], 1)
                act.wait_ge(s_kct[l], 1)
                A(kcT[:], bank[4][:, 0:N_KV * PAST].rearrange("p (g n) -> p g n", g=N_KV), ACT.Copy).then_inc(s_kck[l], 1)
                act.wait_ge(s_v[l], 1)
                act.dma_start(new_v[0, l].rearrange("s g n -> s (g n)"), v_new[:, 0, :]).then_inc(s_kv[l], 16)
                act.wait_ge(s_kn[l], 1)
                act.dma_start(new_k[0, l], k_nat[:, :, 0:HD]).then_inc(s_kv[l], 16)

            def attention(l):
                for s in range(NU + 2):
                    if s < NU:
                        n = N_PROMPT if UNITS[s][0] == 0 else N_SAMPLE + PAST
                        act.wait_ge(s_mx[l], s + 1)
                        if s >= 3:
                            act.wait_ge(s_pt[l], s - 2)
                        A(probs[:, s % 3, 0:n], bank[s % 3][:, 0:n], ACT.Exp, bias=att[:, s % 3, 1:2],
                          scale=HD ** -0.5, accum_out=att[:, s % 3, 2:3]).then_inc(s_ex[l], 1)
                    i = s - 2
                    if i >= 0:
                        n = N_PROMPT if UNITS[i][0] == 0 else N_SAMPLE + PAST
                        act.wait_ge(s_pt[l], i + 1)
                        if i >= 2:
                            act.wait_ge(s_pv[l], i - 1)
                        A(probsT[:, i % 2, 0:n], bank[3 + i % 2][:, 0:n], ACT.Copy).then_inc(s_ptk[l], 1)

            def pooling(l):
                for g in range(NG):
                    act.wait_ge(s_pool_mm[l], g + 1)
                    A(mixT[:, NQ + g, :], bank[g % 2][:, 0:N], ACT.Copy,
                      scale=cols[:, 1, R_PS + l * NG + g:R_PS + l * NG + g + 1]).then_inc(s_pooled[l], 1)

            def up(S, e, w):
                for f in range(NF):
                    act.wait_ge(S["h1"], e * NF + f + 1)
                    if f >= 2:
                        act.wait_ge(S["g"], e * NF + f - 1)
                    A(silu_h[:, f % 2, 0:w], bank[f % 2 * 2][:, 0:w], ACT.Silu).then_inc(S["silu"], 1)

            def keep_y(S, e, w):
                act.wait_ge(S["down"], e * (NF // 2) + NF // 2)
                for s in range(0, w, P):
                    m = min(P, w - s)
                    last = A(y_sb[0:m, s // P, 0:512], bank[6 - s // P * 2][0:m, :], ACT.Copy)
                last.then_inc(S["y_act"], 1)

            for l in range(DEPTH):
                if l == 0:
                    act.wait_ge(s_mod[0], 1)
                norm(2 * l)
                projections(l)
                attention(l)
                pooling(l)
                norm(2 * l + 1)
                act.wait_ge(s_kv[l], 32)
                if l == 0:
                    up(FFN, 0, N)
                    keep_y(FFN, 0, N)
                    act.wait_ge(s_mod[1], 1)
            for t in range(NT):
                act.wait_ge(s_hnt, 2 * t + 1)
                A(h_nat[:, t, 0:512], bank[2 * (t % 2)][:, :], ACT.Copy).then_inc(s_hna, 1)
            act.wait_ge(s_dl, 1)
            A(rsmall[:, 3, :], rsmall[:, 2, :], ACT.Exp).then_inc(s_ed, 1)
            act.wait_ge(s_route, 1)

            def expert(e, w):
                for k in range(0, KD, 2):
                    act.wait_ge(s_gd, e * KD + k + 1)
                    A(heT[:, k, 0:w], bank[k % 4][:, 0:w], ACT.Copy).then_inc(s_ga, 1)
                act.wait_ge(s_gt, e + 1)
                for s in range(0, w, P):
                    m = min(P, w - s)
                    last = A(gatedT[0:m, s // P, :], bank[4 + s // P][0:m, 0:N], ACT.Copy)
                last.then_inc(s_gtk, 1)
                up(MOE, e, w)
                keep_y(MOE, e, w)

            with act.Fori(0, NE) as e:
                by_count(act, e, lambda w: expert(e, w))
            for t in range(NT):
                act.wait_ge(s_yt, 2 * t + 1)
                A(y_sb[:, t, 0:512], bank[2 * t][:, :], ACT.Copy).then_inc(s_ya, 1)

        @blockctx.gpsimd
        def _(pool):
            steps = [0]

            def step(ins):
                steps[0] += 1
                ins.then_inc(s_pool, 1)
                pool.wait_ge(s_pool, steps[0])

            pool.memset(arena[:, 12672:15120], 0.0).then_inc(s_pad, 1)
            tt = nc.gpsimd.tensor_tensor
            for l in range(DEPTH):
                if l == 0:
                    pool.wait_ge(s_mtab, 16)
                for j in range(NQK):
                    pool.wait_ge(s_qn[l], j + 1)
                    if j >= 2:
                        pool.wait_ge(s_qk[l], j - 1)
                    tt(rope_a[:, j % 2, :], qn[:, j, N_PROMPT:N], mtab[:, M_COS:M_COS + N_SAMPLE],
                       ALU.mult).then_inc(s_ra[l], 1)
                for g, w in enumerate(WINDOWS):
                    pool.wait_ge(s_u[l], g + 1)
                    u = upad[:, g, :]
                    lo, hi = 1, PADW
                    step(tt(psum_w[:, 0, lo:hi], u[:, lo - 1:hi - 1], u[:, lo:hi], ALU.add))
                    at, n = 0, 2
                    while n < w:
                        h = n // 2
                        lo, hi = lo + h, hi - h
                        step(tt(psum_w[:, 1 - at, lo:hi], psum_w[:, at, lo - h:hi - h],
                                psum_w[:, at, lo + h:hi + h], ALU.add))
                        at, n = 1 - at, 2 * n
                    for (a, b), p in zip(SEQS, PADDED):
                        last = tt(psum_w[:, 1 - at, p:p + b - a], psum_w[:, at, p:p + b - a],
                                  mtab[:, M_INV + g * N + a:M_INV + g * N + b], ALU.mult)
                    step(last)
                    for (a, b), p in zip(SEQS, PADDED):
                        last = tt(mixT[:, NQ + g, a:b], psum_w[:, 1 - at, p:p + b - a], u[:, p:p + b - a],
                                  ALU.subtract)
                    last.then_inc(s_d[l], 1)
                    pool.wait_ge(s_d[l], g + 1)

        @blockctx.vector
        def _(dve):
            V = nc.vector
            steps = [0]

            def step(ins):
                steps[0] += 1
                ins.then_inc(s_dve, 1)
                dve.wait_ge(s_dve, steps[0])

            for k in range(1, KD, 2):
                dve.wait_ge(s_xt, k + 1)
                V.tensor_copy(xT[:, k, :], bank[k][:, 0:N]).then_inc(s_xv, 1)
            dve.wait_ge(s_colsT, 1)
            V.tensor_copy(cols[:, 0, :], bank[0][:, 0:P]).then_inc(s_cols, 1)
            V.tensor_copy(cols[:, 1, 0:R_END], bank[1][:, 0:R_END]).then_inc(s_cols, 1)
            dve.wait_ge(s_cols, 2)

            def modulation(l):
                dve.wait_ge(s_ada[l], ADA_UNITS)
                step(V.tensor_tensor(mod[:, l, :, :], bank[3][:, 0:2 * MODS].rearrange("p (m c) -> p m c", c=2),
                                     adab(l).unsqueeze(2).to_broadcast((P, MODS, 2)), ALU.add))
                for i in range(2):
                    sc = (1 + 3 * i) * KD
                    last = V.scalar_tensor_tensor(scale_n[:, 2 * l + i], mod[:, l, sc:sc + KD, :], 1.0,
                                                  normw(2 * l + i).unsqueeze(2).to_broadcast((P, KD, 2)),
                                                  ALU.add, ALU.mult)
                last.then_inc(s_mod[l], 1)
                dve.wait_ge(s_mod[l], 1)

            def norm(n):
                dve.wait_ge(s_nss[n], 1)
                V.tensor_scalar(rstd[:], bank[0][:, 0:N], 1.0 / D, EPS, ALU.mult, ALU.add).then_inc(s_nvar[n], 1)
                dve.wait_ge(s_nstd[n], 1)
                step(V.reciprocal(rstd[:], rstd[:]))
                for k in range(KD):
                    V.tensor_tensor(hT[:, k, :], xT[:, k, :], rstd[:], ALU.mult).then_inc(s_nt[n], 1)

            def projections(l):
                dve.wait_ge(s_mtab, 16)
                for j in range(NQK + 2):
                    if j < NQK:
                        dve.wait_ge(s_ss[l], j + 1)
                        V.tensor_scalar(hr[:, j, :], bank[3 + j % 2][:, 0:N], 1.0 / HD, EPS,
                                        ALU.mult, ALU.add).then_inc(s_var[l], 1)
                    i = j - 1
                    if 0 <= i < NQK:
                        dve.wait_ge(s_std[l], i + 1)
                        step(V.reciprocal(hr[:, i, :], hr[:, i, :]))
                        dve.wait_ge(s_raw[l], i + 1)
                        w = (R_QN if i < NQ else R_KN) + l
                        V.scalar_tensor_tensor(qn[:, i, :], raw[:, i, :], cols[:, 1, w:w + 1], hr[:, i, :],
                                               ALU.mult, ALU.mult).then_inc(s_qn[l], 1)
                    i = j - 2
                    if 0 <= i < NQK:
                        dve.wait_ge(s_rot[l], i + 1)
                        step(V.tensor_tensor(rope_b[:, i % 2, :], bank[5 + i % 2][:, 0:N_SAMPLE],
                                             mtab[:, M_SIN:M_SIN + N_SAMPLE], ALU.mult))
                        dve.wait_ge(s_ra[l], i + 1)
                        V.tensor_tensor(qn[:, i, N_PROMPT:N], rope_a[:, i % 2, :], rope_b[:, i % 2, :],
                                        ALU.add).then_inc(s_qk[l], 1)
                dve.wait_ge(s_kt[l], 1)
                V.tensor_copy(k_nat[:], bank[3][:, 0:N_KV * P].rearrange("p (g n) -> p g n", g=N_KV)
                              ).then_inc(s_kn[l], 1)

            def attention(l):
                for s in range(NU + 4):
                    if s < NU:
                        n = N_PROMPT if UNITS[s][0] == 0 else N_SAMPLE + PAST
                        dve.wait_ge(s_sc[l], s + 1)
                        a = att[:, s % 3, :]
                        step(V.reduce_max(a[:, 0:1], bank[s % 3][:, 0:n], AX.X))
                        V.tensor_scalar(a[:, 1:2], a[:, 0:1], -HD ** -0.5, None, ALU.mult).then_inc(s_mx[l], 1)
                    i = s - 1
                    if 0 <= i < NU:
                        n = N_PROMPT if UNITS[i][0] == 0 else N_SAMPLE + PAST
                        dve.wait_ge(s_ex[l], i + 1)
                        a = att[:, i % 3, :]
                        step(V.reciprocal(a[:, 3:4], a[:, 2:3]))
                        V.tensor_scalar(probs[:, i % 3, 0:n], probs[:, i % 3, 0:n], a[:, 3:4], None,
                                        ALU.mult).then_inc(s_pn[l], 1)
                    i = s - 4
                    if i >= 0 and i % 2 == 1:
                        t, h = UNITS[i]
                        dve.wait_ge(s_pv[l], i + 1)
                        V.tensor_copy(mixT[:, h // 2, t * P:(t + 1) * P], bank[5 + i // 2 % 2][:, 0:P]
                                      ).then_inc(s_av[l], 1)

            def add_x(src, ready, first, g, l, done):
                for d in range(KD):
                    dve.wait_ge(ready, first + d + 1)
                    for q, (a, b) in enumerate(SEQS):
                        last = V.scalar_tensor_tensor(xT[:, d, a:b], src(d)[:, a:b], mod[:, l, g + d, q:q + 1],
                                                      xT[:, d, a:b], ALU.mult, ALU.add)
                    last.then_inc(done, 1)

            def up(S, e, w):
                for f in range(NF):
                    dve.wait_ge(S["silu"], e * NF + f + 1)
                    dve.wait_ge(S["h3"], e * NF + f + 1)
                    V.tensor_tensor(gT[:, f, 0:w], silu_h[:, f % 2, 0:w], bank[f % 2 * 2 + 1][:, 0:w],
                                    ALU.mult).then_inc(S["g"], 1)

            def keep_y(S, e, w):
                dve.wait_ge(S["down"], e * (NF // 2) + NF // 2)
                for s in range(0, w, P):
                    m = min(P, w - s)
                    last = V.tensor_copy(y_sb[0:m, s // P, 512:D], bank[7 - s // P * 2][0:m, :])
                last.then_inc(S["y_dve"], 1)

            def routing():
                r = lambda i: rt[:, i, :, :]
                m = lambda i: rsmall[:, i, :]
                wide = lambda v: v.unsqueeze(2).to_broadcast((P, NT, NE))
                L, eq, key, sel1, L2, sel2, sel, g1, g2, gate = (r(i) for i in (0, 1, 2, 3, 4, 5, 10, 6, 7, 8))
                rk = rank.unsqueeze(1).to_broadcast((P, NT, NE))
                dve.wait_ge(s_lg, 1)
                step(V.tensor_copy(L, bank[4][:, 0:NT * NE].rearrange("p (t n) -> p t n", t=NT)))
                for t in range(NT):
                    dve.wait_ge(s_hnt, 2 * t + 2)
                    V.tensor_copy(h_nat[:, t, 512:D], bank[2 * (t % 2) + 1][:, :]).then_inc(s_hnv, 1)

                def first_largest(x, largest, out):
                    step(V.reduce_max(largest, x, AX.X))
                    step(V.tensor_tensor(eq, x, wide(largest), ALU.is_equal))
                    step(V.tensor_tensor(key, eq, rk, ALU.mult))
                    step(V.reduce_max(m(5), key, AX.X))
                    step(V.tensor_tensor(out, key, wide(m(5)), ALU.is_equal))

                first_largest(L, m(0), sel1)
                step(V.scalar_tensor_tensor(L2, sel1, -3.0e38, L, ALU.mult, ALU.add))
                first_largest(L2, m(1), sel2)
                V.tensor_tensor(sel, sel1, sel2, ALU.add).then_inc(s_sel, 1)
                V.tensor_tensor(m(2), m(1), m(0), ALU.subtract).then_inc(s_dl, 1)
                dve.wait_ge(s_ed, 1)
                step(V.tensor_scalar(m(4), m(3), 1.0, None, ALU.add))
                step(V.reciprocal(m(6), m(4)))
                step(V.tensor_tensor(m(7), m(6), m(3), ALU.mult))
                V.tensor_tensor(g1, sel1, wide(m(6)), ALU.mult)
                step(V.tensor_tensor(g2, sel2, wide(m(7)), ALU.mult))
                by_expert = lambda i: route[:, :, i, :].rearrange("p e t -> p t e")
                V.tensor_tensor(by_expert(1), g1, g2, ALU.add)
                dve.wait_ge(s_sel, 1)
                dve.wait_ge(s_posd, 1)
                step(V.scalar_tensor_tensor(r(9), bank[5][:, 0:NT * NE].rearrange("p (t n) -> p t n", t=NT), 1.0,
                                            sel, ALU.add, ALU.mult))
                V.tensor_scalar(by_expert(0), r(9), -1.0, None, ALU.add)
                V.tensor_copy(counts[:], bank[6][0:1, 0:NE]).then_inc(s_route, 1)
                dve.wait_ge(s_route, 1)

            def expert(e, w):
                V.tensor_copy(cur[:].rearrange("p (o i t) -> p o i t", o=1, i=2), route[:, ds(e, 1), :, :]
                              ).then_inc(s_cur, 1)
                dve.wait_ge(s_cur, e + 1)
                for t in range(NT):
                    last = V.tensor_scalar(onehot[:, t, 0:w], iota[:, 0:w], cur[:, t:t + 1], None, ALU.is_equal)
                last.then_inc(s_oh, 1)
                for t in range(NT):
                    last = V.tensor_scalar(gated[:, t, 0:w], iota[:, 0:w], cur[:, t:t + 1],
                                           cur[:, NT + t:NT + t + 1], ALU.is_equal, ALU.mult)
                last.then_inc(s_oh, 1)
                for k in range(1, KD, 2):
                    dve.wait_ge(s_gd, e * KD + k + 1)
                    V.tensor_copy(heT[:, k, 0:w], bank[k % 4][:, 0:w]).then_inc(s_gv, 1)
                up(MOE, e, w)
                keep_y(MOE, e, w)
                dve.wait_ge(s_xadd, e * KD + KD)
                add_x(lambda d: bank[4 + d % 4], MOE["back"], e * KD, 5 * KD, 1, MOE["x_add"])

            for l in range(DEPTH):
                modulation(l)
                norm(2 * l)
                projections(l)
                attention(l)
                add_x(lambda d: bank[2 + d % 4], s_wo[l], 0, 2 * KD, l, s_x1[l])
                norm(2 * l + 1)
                dve.wait_ge(s_kv[l], 32)
                if l == 0:
                    up(FFN, 0, N)
                    keep_y(FFN, 0, N)
                    add_x(lambda d: bank[4 + d % 4], FFN["back"], 0, 5 * KD, 0, FFN["x_add"])
            routing()
            with dve.Fori(0, NE) as e:
                by_count(dve, e, lambda w: expert(e, w))
            for t in range(NT):
                dve.wait_ge(s_yt, 2 * t + 2)
                V.tensor_copy(y_sb[:, t, 512:D], bank[2 * t + 1][:, :]).then_inc(s_yv, 1)


_INS = ("x_prompt", "x_sample", "cache_k", "cache_v", "c", "c_ctx", "norm1_w", "norm2_w", "ada_w", "ada_b",
        "w_in", "w_o", "q_norm_w", "k_norm_w", "pool_w", "pool_scale", "ffn_w1", "ffn_w3", "ffn_w2",
        "router_w", "router_b", "moe_w1", "moe_w3", "moe_w2")
_OUTS = ((1, N_PROMPT, D), (1, N_SAMPLE, D), (1, DEPTH, N_PROMPT, N_KV, HD), (1, DEPTH, N_PROMPT, N_KV, HD))


def kernel(**inputs):
    import concourse.bacc as bacc
    from concourse.bass_utils import run_bass_kernel_spmd

    nc = bacc.Bacc("TRN2", target_bir_lowering=False, num_devices=1)
    arrays, args = {}, []
    tables = dict(zip(("const_tab", "mix_tab"), constants()))
    for name in _INS + tuple(tables):
        a = np.ascontiguousarray(tables[name] if name in tables else inputs[name])
        arrays[f"in_{name}"] = a
        args.append(nc.dram_tensor(f"in_{name}", a.shape, mybir.dt.from_np(a.dtype), kind="ExternalInput").ap())
    for i, shape in enumerate(_OUTS):
        args.append(nc.dram_tensor(f"out_{i}", shape, mybir.dt.float32, kind="ExternalOutput").ap())
    build(nc, *args)
    r = run_bass_kernel_spmd(nc, [arrays], core_ids=[0])
    return tuple(r.results[0][f"out_{i}"] for i in range(len(_OUTS)))
```

```python
import concourse.bass as bass
from concourse import mybir
from contextlib import ExitStack
import numpy as np

P = 128
D = 1024
KD = D // P
DEPTH = 2
N_PROMPT, N_SAMPLE, PAST = 128, 256, 128
N = N_PROMPT + N_SAMPLE
NT = N // P
HD = 64
N_HEADS, N_KV = 8, 2
ATTN = N_HEADS * HD
KV_W = N_KV * HD
POOL_W = D - ATTN
WINDOWS = (2, 4, 8, 16)
NG = len(WINDOWS)
IN_COLS = ATTN + 2 * KV_W + POOL_W
FF = 2816
NF = FF // P
NE = 8
GRID_W = 64
THETA = 10000.0
EPS = 1e-6
SLOTS = 6
SPLIT = 3
UCOLS = 256
UNIT = KD * UCOLS
MODS = 6 * KD
ADA_UNITS = 6 * D // UCOLS
MIX_UNITS = 6 + D // UCOLS
GROUPS = NF // 2
FF_UNITS = 3 * GROUPS
LOADS = ([(0, 0), (0, 1)] + [(g + (k < 2), k) for g in range(GROUPS - 1) for k in range(3)]
         + [(GROUPS - 1, 2)])
ITEM = 6
NQ = ATTN // P
NQK = NQ + N_KV
PAD = max(WINDOWS) // 2
PADW = PAD + N_PROMPT + PAD + N_SAMPLE + PAD
SEQS = ((0, N_PROMPT), (N_PROMPT, N))
PADDED = (PAD, 2 * PAD + N_PROMPT)
UNITS = [(t, h) for t in range(NT) for h in range(N_HEADS)]
NU = len(UNITS)

C_ID, C_ONE, C_BLK, C_PERM, C_TRI = 0, P, 2 * P, 3 * P, 4 * P
C_IOTA = 5 * P
C_RANK = C_IOTA + N
C_SEL = C_RANK + NE
N_CONST = C_SEL + 2
M_COS, M_SIN, M_INV = 0, N_SAMPLE, 2 * N_SAMPLE
N_MTAB = M_INV + NG * N


def constants():
    c = np.zeros((P, N_CONST), np.float32)
    i = np.arange(P)
    c[:, C_ID:C_ID + P] = np.eye(P)
    c[:, C_ONE:C_ONE + P] = 1.0
    c[:, C_BLK:C_BLK + P] = (i[:, None] // HD == i[None, :] // HD)
    nf = HD // 4
    half = (i // nf) % 2
    partner = np.where(half == 0, i + nf, i - nf)
    c[partner, C_PERM + i] = np.where(half == 0, -1.0, 1.0)
    c[:, C_TRI:C_TRI + P] = (i[:, None] < i[None, :])
    c[:, C_IOTA:C_IOTA + N] = np.arange(N)[None, :]
    c[:, C_RANK:C_RANK + NE] = (NE - np.arange(NE))[None, :]
    for j in range(4):
        c[32 * j, C_SEL] = c[32 * j + 1, C_SEL + 1] = 1.0
    m = np.zeros((P, N_MTAB), np.float32)
    inv = (np.float32(THETA) ** (-np.arange(nf, dtype=np.float32) / np.float32(nf))).astype(np.float32)
    t = np.arange(N_SAMPLE)
    pos = np.stack([(t // GRID_W), (t % GRID_W)]).astype(np.float32)
    ang = pos[(i % HD) // (2 * nf)] * inv[i % nf][:, None]
    m[:, M_COS:M_COS + N_SAMPLE] = np.cos(ang)
    m[:, M_SIN:M_SIN + N_SAMPLE] = np.sin(ang)
    for g, w in enumerate(WINDOWS):
        for a, b in SEQS:
            n = b - a
            k = np.arange(n)
            cnt = np.clip(k + w // 2, 0, n) - np.clip(k - w // 2, 0, n)
            m[:, M_INV + g * N + a:M_INV + g * N + b] = (1.0 / cnt.astype(np.float32))[None, :]
    return c, m


def build(nc, x_prompt, x_sample, cache_k, cache_v, c, c_ctx, norm1_w, norm2_w, ada_w, ada_b,
          w_in, w_o, q_norm_w, k_norm_w, pool_w, pool_scale, ffn_w1, ffn_w3, ffn_w2,
          router_w, router_b, moe_w1, moe_w3, moe_w2, const_tab, mix_tab,
          y_prompt, y_sample, new_k, new_v):
    f32 = mybir.dt.float32
    f32r = mybir.dt.float32r
    i32 = mybir.dt.int32
    ALU = mybir.AluOpType
    ACT = mybir.ActivationFunctionType
    AX = mybir.AxisListType
    ds = bass.ds

    ctx = ExitStack()
    with ctx:
        def sb(name, shape, dt=f32):
            return ctx.enter_context(nc.sbuf_tensor(name, shape, dt))

        def sem(name):
            return ctx.enter_context(nc.semaphore(name))

        ring = sb("ring", [P, SLOTS, UNIT])
        w_hi = sb("w_hi", [P, SPLIT, UNIT], f32r)
        w_lo = sb("w_lo", [P, SPLIT, UNIT], f32r)
        xT = sb("xT", [P, KD, N])
        a_hi = sb("a_hi", [P, KD, N], f32r)
        a_lo = sb("a_lo", [P, KD, N], f32r)
        g_hi = sb("g_hi", [P, 2, P], f32r)
        g_lo = sb("g_lo", [P, 2, P], f32r)
        arena = sb("arena", [P, 12432])
        tables = sb("tables", [P, N_MTAB + DEPTH * NG * P])
        small = sb("small", [P, 2 * P + 11 * NT * NE])
        const = sb("const", [P, N_CONST])
        cols = sb("cols", [P, 2, P])
        cond32 = sb("cond32", [P, KD, 32])
        mod = sb("mod", [P, DEPTH, MODS, 2])
        scale_n = sb("scale_n", [P, 2 * DEPTH, KD, 2])
        rstd = sb("rstd", [P, N])
        att = sb("att", [P, 3, 4])
        rsmall = sb("rsmall", [P, 8, NT])
        rw = sb("rw", [P, KD, NE])
        rb = sb("rb", [1, NE])
        route = sb("route", [P, NE + 1, 2, NT])
        cur = sb("cur", [P, 2 * NT])
        counts = sb("counts", [1, NE + 1], i32)

        def part(t, at, *dims):
            n = int(np.prod(dims))
            v = t[:, at:at + n]
            if len(dims) == 2:
                return v.rearrange("p (a b) -> p a b", a=dims[0])
            if len(dims) == 3:
                return v.rearrange("p (a b c) -> p a b c", a=dims[0], b=dims[1])
            return v

        rows = part(small, 0, 2, P)
        rt = part(small, 2 * P, 11, NT, NE)
        x_nat = part(arena, 0, NT, D)
        hf = part(arena, 0, KD, N)
        ada_part = part(arena, 3072, 2, UCOLS)
        qn = part(arena, 0, NQK, N)
        raw = part(arena, 2304, 3, N)
        sq = part(arena, 3456, 3, N)
        hr = part(arena, 4608, 2, N)
        v_new = part(arena, 5376, NT, KV_W)
        vT = part(arena, 5760, N)
        diff = part(arena, 6144, NG, N)
        upad = part(arena, 7680, NG, PADW)
        win = part(arena, 9312, 2, PADW)
        rope_a = part(arena, 10128, 2, N_SAMPLE)
        rope_b = part(arena, 10640, 2, N_SAMPLE)
        k_nat = part(arena, 11152, N_KV, P)
        kc_nat = part(arena, 11408, DEPTH, N_KV * P)
        vc = part(arena, 11920, DEPTH, KV_W)
        kcT = part(arena, 12176, N_KV, PAST)
        probs, probsT = raw, sq
        y_sb = part(arena, 0, NT, D)
        g_nat = part(arena, 3072, UCOLS)
        silu_h = part(arena, 3328, UCOLS)
        h_nat = part(arena, 3584, NT, D)
        onehot = part(arena, 6656, NT, N)
        gated = part(arena, 7808, NT, N)
        gatedT = [part(arena, 8960, NT, N), part(arena, 10112, NT, N)]
        mtab = part(tables, 0, N_MTAB)
        pw = part(tables, N_MTAB, DEPTH * NG, P)

        bank = [ctx.enter_context(nc.psum_tensor(f"bank{i}", [P, 512], f32)) for i in range(8)]
        ident = const[:, C_ID:C_ID + P]
        ones = const[:, C_ONE:C_ONE + P]
        blocks = const[:, C_BLK:C_BLK + P]
        perm = const[:, C_PERM:C_PERM + P]
        tri = const[:, C_TRI:C_TRI + P]
        iota = const[:, C_IOTA:C_IOTA + N]
        rank = const[:, C_RANK:C_RANK + NE]
        cond_sel = const[:, C_SEL:C_SEL + 2]
        R_CTX, R_C, R_PS, R_QN, R_KN, R_END = 0, KD, 2 * KD, 2 * KD + DEPTH * NG, 2 * KD + DEPTH * NG + 2, 2 * KD + DEPTH * NG + 4

        def adab(l):
            return cols[:, 0, l * MODS:(l + 1) * MODS]

        def normw(n):
            a = DEPTH * MODS + (n % 2) * DEPTH * KD + (n // 2) * KD
            return cols[:, 0, a:a + KD]

        slot_full = [sem(f"slot_full{s}") for s in range(SLOTS)]
        A0 = [0, ADA_UNITS + MIX_UNITS + FF_UNITS]
        M0 = [a + ADA_UNITS for a in A0]
        F0 = [m + MIX_UNITS for m in M0]

        def slot(i):
            return ring[:, i % SLOTS, :]

        def block(i):
            return slot(i).rearrange("p (k n) -> p k n", k=KD)

        def loads(i):
            def n(u):
                for l in range(DEPTH):
                    if u == M0[l] + 2:
                        return 4
                    if u >= F0[l] and (l == 1 or u < F0[0] + FF_UNITS):
                        return 2 if LOADS[(u - F0[l]) % FF_UNITS][1] < 2 else 1
                return 1
            return sum(n(u) for u in range(i % SLOTS, i + 1, SLOTS))

        def wait_unit(eng, i, turns=0):
            if isinstance(turns, int):
                eng.wait_ge(slot_full[i % SLOTS], 16 * loads(i))
            else:
                per_turn = loads(i + 2 * FF_UNITS) - loads(i)
                eng.wait_ge(slot_full[i % SLOTS], turns * (16 * per_turn) + 16 * (loads(i) - per_turn))

        def split_no(i):
            for l in range(DEPTH):
                if M0[l] <= i < F0[l]:
                    return i - (l + 1) * ADA_UNITS
            l = 0 if i < A0[1] else 1
            part, j = divmod(i - F0[l], FF_UNITS)
            return F0[l] - (l + 1) * ADA_UNITS + part * FF_UNITS + LOADS[j][0] * 3 + LOADS[j][1]

        def unit(F, g, kind):
            return F + LOADS.index((g, kind))

        def split_count(sems, i, turns=0):
            n = split_no(i) // SPLIT + 1
            per_turn = 2 * FF_UNITS // SPLIT
            return sems[split_no(i) % SPLIT], n if isinstance(turns, int) else turns * per_turn + (n - per_turn)

        def hi_of(i):
            return w_hi[:, split_no(i) % SPLIT, :]

        def lo_of(i):
            return w_lo[:, split_no(i) % SPLIT, :]

        s_x, s_const, s_mtab, s_rows, s_pw, s_cache, s_router = map(
            sem, ("x_in", "const_in", "mtab_in", "rows_in", "pw_in", "cache_in", "router_in"))
        s_xt, s_xa, s_xv = sem("x_transposed"), sem("x_kept_act"), sem("x_kept_dve")
        s_colsT, s_cols, s_cond = sem("cols_transposed"), sem("cols_kept"), sem("cond_silu")
        s_pad = sem("pads_zeroed")
        s_dve, s_act, s_pool = sem("dve_step"), sem("act_step"), sem("pool_step")
        per = lambda name, n=DEPTH: [sem(f"{name}{i}") for i in range(n)]
        s_ada, s_mod, s_apk, s_apm = per("ada_done"), per("mod_ready"), per("ada_kept"), per("ada_summed")
        s_c0 = sem("cond_zeroed")
        s_hi, s_lo = per("weights_hi", SPLIT), per("weights_lo", SPLIT)
        s_naf, s_nhi = sem("norm_affine"), sem("norm_hi")
        s_nsq, s_nss, s_nvar, s_nstd, s_nt, s_nh = map(sem, (
            "norm_squares", "norm_sum", "norm_var", "norm_std", "norm_scaled", "norm_out"))
        s_proj, s_raw, s_sq, s_ss = per("proj_done"), per("raw_kept"), per("squares"), per("head_sum")
        s_var, s_std, s_qn, s_rot, s_ra, s_qk = (per(n) for n in (
            "head_var", "head_std", "head_normed", "rotated", "rope_cos", "qk_ready"))
        s_u, s_v, s_kt, s_kn = per("u_kept"), per("v_kept"), per("k_transposed"), per("k_nat_kept")
        s_kct, s_kck = per("cache_transposed"), per("cache_kept")
        s_d, s_pool_mm, s_pooled, s_pool_hi = per("pool_diff"), per("pool_product"), per("pooled"), per("pooled_hi")
        s_vT, s_vn = per("vT_kept"), per("v_transposed")
        s_sc, s_mx, s_ex, s_pn, s_pt, s_ptk, s_pv, s_av = (per(n) for n in (
            "scores", "score_max", "probs_exp", "probs_normed", "probs_transposed", "probsT_kept",
            "pv_done", "attn_kept"))
        s_ah = per("attn_hi")
        s_wo, s_x1 = per("wo_done"), per("x_after_mixer")
        s_out, s_kv = sem("stores"), per("kv_stores")
        S = {n: sem(f"ff_{n}") for n in ("first", "up", "silu", "mul", "tr", "g_hi", "g_lo", "down",
                                          "y_act", "y_dve", "back", "x_add")}

        def item(part, g, s, ns):
            return part * (ITEM * GROUPS) + ITEM * g + (s + 1) * (ITEM // ns)

        s_hnt, s_hna, s_hnv = sem("h_nat_transposed"), sem("h_nat_act"), sem("h_nat_dve")
        s_lg, s_dl, s_ed, s_sel, s_posd, s_route = map(sem, (
            "logits", "top2_gap", "top2_exp", "selected", "positions", "routed"))
        s_cur, s_oh, s_gd, s_ga, s_gv, s_gt, s_gtk = map(sem, (
            "cur_copied", "onehot_ready", "gathered", "gathered_act", "gathered_dve",
            "gate_transposed", "gateT_kept"))
        s_yt, s_ya, s_yv = sem("y_transposed"), sem("y_kept_act"), sem("y_kept_dve")

        N_ROW_LOADS, N_CACHE_LOADS = 10, 3 * DEPTH

        def by_count(eng, e, body, none=False):
            n = eng.value_load(counts[:, e if isinstance(e, slice) else ds(e, 1)], min_val=0, max_val=N + 1)
            with eng.If(n <= P):
                body(1)
            with eng.Else():
                with eng.If(n <= 2 * P):
                    body(2)
                with eng.Else():
                    if not none:
                        body(3)
                    else:
                        with eng.If(n <= N):
                            body(3)
                        with eng.Else():
                            body(0)

        def gather_banks(ns):
            return ((0, 2, 3, 4, 5), (0, 2, 3), (0,))[ns - 1]

        def gather_sets(ns, banks):
            n = (4, 2, 1)[ns - 1]
            return [(range(j * n, j * n + n), banks[j % len(banks)]) for j in range(KD // n)]

        blockctx = ctx.enter_context(nc.Block())

        @blockctx.sync
        def _(sp):
            def free(i):
                u = i - SLOTS
                if u < 0:
                    return
                for l in range(DEPTH):
                    if A0[l] <= u < M0[l]:
                        sp.wait_ge(s_ada[l], u - A0[l] + 1)
                        return
                sp.wait_ge(*split_count(s_lo, u))

            def columns(i, w, a, n=UCOLS):
                free(i)
                sp.dma_start(block(i)[:, :, 0:n],
                             w[:, a:a + n].rearrange("(k p) n -> p k n", p=P)).then_inc(slot_full[i % SLOTS], 16)

            def ff_unit(i, j, w1, w3, w2):
                g, kind = LOADS[j]
                full = slot_full[i % SLOTS]
                if kind < 2:
                    dst = slot(i).rearrange("p (k m n) -> p k m n", k=KD // 2, m=2)
                    r = kind * (D // 2)
                    for m, w in enumerate((w1, w3)):
                        sp.dma_start(dst[:, :, m, :], w[r:r + D // 2, g * UCOLS:(g + 1) * UCOLS].rearrange(
                            "(k p) n -> p k n", p=P)).then_inc(full, 16)
                else:
                    sp.dma_start(slot(i).rearrange("p (f n) -> p f n", f=2),
                                 w2[g * 2 * P:(g + 1) * 2 * P, :].rearrange("(f p) n -> p f n", p=P)).then_inc(full, 16)

            for l in range(DEPTH):
                for u in range(ADA_UNITS):
                    columns(A0[l] + u, ada_w[l], u * UCOLS)
                m = M0[l]
                columns(m, w_in[l], 0)
                columns(m + 1, w_in[l], UCOLS)
                free(m + 2)
                dst = block(m + 2).rearrange("p k (g r n) -> p k g r n", g=N_KV, r=2)
                for g in range(N_KV):
                    src = w_in[l][:, ATTN + g * HD:ATTN + (g + 1) * HD].rearrange("(k p) n -> p k n", p=P)
                    for r in range(2):
                        sp.dma_start(dst[:, :, g, r, :], src).then_inc(slot_full[(m + 2) % SLOTS], 16)
                columns(m + 3, w_in[l], ATTN + 2 * KV_W)
                columns(m + 4, w_in[l], ATTN + 2 * KV_W + UCOLS)
                columns(m + 5, w_in[l], ATTN + KV_W, KV_W)
                for u in range(D // UCOLS):
                    columns(m + 6 + u, w_o[l], u * UCOLS)
                if l == 0:
                    for j in range(FF_UNITS):
                        free(F0[0] + j)
                        ff_unit(F0[0] + j, j, ffn_w1[0], ffn_w3[0], ffn_w2[0])
            sp.wait_ge(*split_count(s_lo, F0[1] - 1))
            with sp.Fori(1, NE // 2 + 1) as turn:
                for q in range(2):
                    w1, w3, w2 = (w[0, ds(2 * turn - 2 + q, 1)].rearrange("o k n -> (o k) n")
                                  for w in (moe_w1, moe_w3, moe_w2))
                    for j in range(FF_UNITS):
                        i = F0[1] + q * FF_UNITS + j
                        if i - SLOTS < F0[1]:
                            sp.wait_ge(*split_count(s_lo, i - SLOTS + 2 * FF_UNITS, turn - 1))
                        else:
                            sp.wait_ge(*split_count(s_lo, i - SLOTS, turn))
                        ff_unit(i, j, w1, w3, w2)
            sp.wait_ge(s_ya, NT)
            sp.wait_ge(s_yv, NT)
            sp.dma_start(y_prompt[0], y_sb[:, 0, :]).then_inc(s_out, 16)
            sp.dma_start(y_sample[0].rearrange("(t p) d -> p t d", p=P), y_sb[:, 1:NT, :]).then_inc(s_out, 16)
            sp.wait_ge(s_out, 32)
            for l in range(DEPTH):
                sp.wait_ge(s_kv[l], 32)

        @blockctx.tensor
        def _(pe):
            mm, tr = nc.tensor.matmul, nc.tensor.transpose

            pe.wait_ge(s_const, 16)
            pe.wait_ge(s_x, 32)
            for k in range(KD):
                for t in range(NT):
                    last = tr(bank[k][:, t * P:(t + 1) * P], x_nat[:, t, k * P:(k + 1) * P], ident)
                last.then_inc(s_xt, 1)
            pe.wait_ge(s_rows, 16 * N_ROW_LOADS)
            pe.wait_ge(s_xa, 1)
            tr(bank[0][:, 0:P], rows[:, 0, :], ident)
            pe.wait_ge(s_xv, 1)
            tr(bank[1][:, 0:R_END], rows[0:R_END, 1, :], ident[0:R_END, 0:R_END]).then_inc(s_colsT, 1)

            def three(out, a_hi_, a_lo_, b_hi_, b_lo_, first, last):
                mm(out, a_hi_, b_hi_, start=first, stop=False)
                mm(out, a_hi_, b_lo_, start=False, stop=False)
                return mm(out, a_lo_, b_hi_, start=False, stop=last)

            def wait_split(i, turns=0):
                pe.wait_ge(*split_count(s_lo, i, turns))

            def split_block(t, i):
                return t(i).rearrange("p (k n) -> p k n", k=KD)

            def ada(l):
                if l == 1:
                    pe.wait_ge(S["x_add"], 6)
                if l == 0:
                    pe.wait_ge(s_cond, 1)
                    pe.wait_ge(s_xv, 4)
                    pe.wait_ge(s_xa, 4)
                for u in range(ADA_UNITS + 1):
                    if u < ADA_UNITS:
                        wait_unit(pe, A0[l] + u)
                        if u >= 2:
                            pe.wait_ge(s_apk[l], u - 1)
                        w = block(A0[l] + u)
                        for k in range(KD):
                            j = 32 * (k % 4)
                            last = mm(bank[4 + u % 2][j:j + 32, 0:UCOLS], cond32[:, k, :], w[:, k, :],
                                      start=(k < 4), stop=(k >= 4))
                        last.then_inc(s_ada[l], 1)
                    if u >= 1:
                        pe.wait_ge(s_apk[l], u)
                        for c2 in range(2):
                            at = 2 * (2 * (u - 1) + c2)
                            last = mm(bank[3][:, at:at + 2], ada_part[:, (u - 1) % 2, c2 * P:(c2 + 1) * P],
                                      cond_sel, start=True, stop=True)
                        last.then_inc(s_apm[l], 1)

            def norm(n):
                for k in range(KD):
                    pe.wait_ge(s_nsq, n * KD + k + 1)
                    last = mm(bank[0][:, 0:N], ones, hf[:, k, :], start=(k == 0), stop=(k == KD - 1))
                last.then_inc(s_nss, 1)

            def projections(l):
                m = M0[l]
                nchunk = NQK + NG + 1
                for j in range(nchunk + 3):
                    if j < nchunk:
                        u = m + j // 2
                        if j % 2 == 0:
                            wait_split(u)
                        wh, wl = split_block(hi_of, u), split_block(lo_of, u)
                        if 3 <= j < NQK + 3:
                            pe.wait_ge(s_sq[l], j - 2)
                        elif j >= NQK + 3:
                            pe.wait_ge(s_u[l], j - 2 - NQK)
                        n = slice(j % 2 * P, (j % 2 + 1) * P)
                        for k in range(KD):
                            if j == 0:
                                pe.wait_ge(s_nh, 2 * l * KD + k + 1)
                            last = three(bank[j % 3][:, 0:N], wh[:, k, n], wl[:, k, n], a_hi[:, k, :], a_lo[:, k, :],
                                         k == 0, k == KD - 1)
                        last.then_inc(s_proj[l], 1)
                    i = j - 1
                    if 0 <= i < NQK:
                        pe.wait_ge(s_sq[l], i + 1)
                        if i >= 2:
                            pe.wait_ge(s_var[l], i - 1)
                        mm(bank[3 + i % 2][:, 0:N], blocks, sq[:, i % 3, :], start=True, stop=True).then_inc(s_ss[l], 1)
                    i = j - 3
                    if 0 <= i < NQK:
                        pe.wait_ge(s_qn[l], i + 1)
                        if i >= 2:
                            pe.wait_ge(s_qk[l], i - 1)
                        mm(bank[5 + i % 2][:, 0:N_SAMPLE], perm, qn[:, i, N_PROMPT:N],
                           start=True, stop=True).then_inc(s_rot[l], 1)
                pe.wait_ge(s_vT[l], 1)
                for t in range(NT):
                    last = tr(bank[0][:, t * KV_W:(t + 1) * KV_W], vT[:, t * P:(t + 1) * P], ident)
                last.then_inc(s_vn[l], 1)
                pe.wait_ge(s_var[l], NQK)
                for g in range(N_KV):
                    last = tr(bank[3][:, g * P:(g + 1) * P], qn[:, NQ + g, 0:N_PROMPT], ident)
                last.then_inc(s_kt[l], 1)
                pe.wait_ge(s_cache, 16 * N_CACHE_LOADS)
                for g in range(N_KV):
                    last = tr(bank[4][:, g * P:(g + 1) * P], kc_nat[:, l, g * P:(g + 1) * P], ident)
                last.then_inc(s_kct[l], 1)

            def pooling(l):
                pe.wait_ge(s_pw, 16)
                for g in range(NG):
                    pe.wait_ge(s_d[l], g + 1)
                    if g == 0:
                        pe.wait_ge(s_av[l], NU // 2)
                    if g >= 2:
                        pe.wait_ge(s_pooled[l], g - 1)
                    mm(bank[g % 2][:, 0:N], pw[:, l * NG + g, :], diff[:, g, :],
                       start=True, stop=True).then_inc(s_pool_mm[l], 1)

            def attention(l):
                pe.wait_ge(s_qk[l], NQK)
                pe.wait_ge(s_kck[l], 1)
                pe.wait_ge(s_v[l], 1)
                pe.wait_ge(s_kn[l], 1)
                for s in range(NU + 3):
                    if s < NU:
                        t, h = UNITS[s]
                        g, a = h // (N_HEADS // N_KV), h % 2 * HD
                        if s >= 3:
                            pe.wait_ge(s_ex[l], s - 2)
                        b = bank[s % 3]
                        q = qn[a:a + HD, h // 2, t * P:(t + 1) * P]
                        k = qn[a:a + HD, NQ + g, :]
                        if t == 0:
                            last = mm(b[:, 0:N_PROMPT], q, k[:, 0:N_PROMPT], start=True, stop=True)
                        else:
                            mm(b[:, 0:N_SAMPLE], q, k[:, N_PROMPT:N], start=True, stop=True)
                            last = mm(b[:, N_SAMPLE:N_SAMPLE + PAST], q, kcT[a:a + HD, g, :], start=True, stop=True)
                        last.then_inc(s_sc[l], 1)
                    i = s - 2
                    if 0 <= i < NU:
                        t, h = UNITS[i]
                        pe.wait_ge(s_pn[l], i + 1)
                        if i >= 2:
                            pe.wait_ge(s_ptk[l], i - 1)
                        for kt in range(1 if t == 0 else NT):
                            last = tr(bank[3 + i % 2][:, kt * P:(kt + 1) * P],
                                      probs[:, i % 3, kt * P:(kt + 1) * P], ident)
                        last.then_inc(s_pt[l], 1)
                    i = s - 3
                    if 0 <= i < NU:
                        t, h = UNITS[i]
                        g, a = h // (N_HEADS // N_KV), h % 2 * HD
                        pe.wait_ge(s_ptk[l], i + 1)
                        if i >= 4 and i % 2 == 0:
                            pe.wait_ge(s_av[l], i // 2 - 1)
                        b = bank[5 + i // 2 % 2]
                        vs = [v_new[:, 0, :]] if t == 0 else [v_new[:, 1, :], v_new[:, 2, :], vc[:, l, :]]
                        for kt, v in enumerate(vs):
                            last = mm(b[a:a + HD, 0:P], v[:, g * HD:(g + 1) * HD],
                                      probsT[:, i % 2, kt * P:(kt + 1) * P],
                                      start=(kt == 0), stop=(kt == len(vs) - 1))
                        last.then_inc(s_pv[l], 1)

            def output(l):
                pe.wait_ge(s_pooled[l], NG)
                for d in range(KD):
                    i = M0[l] + 6 + d // 2
                    if d % 2 == 0:
                        wait_split(i)
                    if d >= 4:
                        pe.wait_ge(s_x1[l], d - 3)
                    wh, wl = split_block(hi_of, i), split_block(lo_of, i)
                    n = slice(d % 2 * P, (d % 2 + 1) * P)
                    for k in range(KD):
                        last = three(bank[2 + d % 4][:, 0:N], wh[:, k, n], wl[:, k, n], a_hi[:, k, :], a_lo[:, k, :],
                                     k == 0, k == KD - 1)
                    last.then_inc(s_wo[l], 1)

            def feed_forward(part, F, turns, ns):
                def down(g, s):
                    B = unit(F, g, 2)
                    if s == 0:
                        wait_split(B, turns)
                    pe.wait_ge(S["g_lo"], item(part, g, s, ns))
                    wh, wl = (t(B).rearrange("p (f n) -> p f n", f=2) for t in (hi_of, lo_of))
                    for f in range(2):
                        for a_, w_ in ((g_hi, wh), (g_hi, wl), (g_lo, wh)):
                            for half in range(2):
                                first = g == 0 and f == 0 and a_ is g_hi and w_ is wh
                                final = g == GROUPS - 1 and f == 1 and a_ is g_lo
                                last = mm(bank[6 - 2 * s + half][:, :], a_[:, f, :],
                                          w_[:, f, half * 512:(half + 1) * 512], start=first, stop=final)
                    last.then_inc(S["down"], ITEM // ns)

                before = None
                for g in range(GROUPS):
                    for s in range(ns):
                        for k in range(KD):
                            U = unit(F, g, k // 4)
                            if s == 0 and k % 4 == 0:
                                wait_split(U, turns)
                            wh, wl = (t(U).rearrange("p (k n) -> p k n", k=KD // 2)[:, k % 4, :]
                                      for t in (hi_of, lo_of))
                            tile = slice(s * P, (s + 1) * P)
                            last = three(bank[0][:, :], a_hi[:, k, tile], a_lo[:, k, tile], wh, wl,
                                         k == 0, k == KD - 1)
                            if k == 3 and s == ns - 1:
                                last.then_inc(S["first"], 1)
                        last.then_inc(S["up"], ITEM // ns)
                        if before:
                            down(*before)
                        pe.wait_ge(S["mul"], item(part, g, s, ns))
                        for f in range(2):
                            last = tr(bank[1][:, f * P:(f + 1) * P], g_nat[:, f * P:(f + 1) * P], ident)
                        last.then_inc(S["tr"], ITEM // ns)
                        before = (g, s)
                return lambda: down(*before)

            def dense():
                feed_forward(0, F0[0], 0, NT)()
                pe.wait_ge(S["y_act"], 1)
                pe.wait_ge(S["y_dve"], 1)
                for d in range(KD):
                    if d >= 4:
                        pe.wait_ge(S["x_add"], d - 3)
                    for t in range(NT):
                        last = tr(bank[4 + d % 4][:, t * P:(t + 1) * P], y_sb[:, t, d * P:(d + 1) * P], ident)
                    last.then_inc(S["back"], 1)

            def routing():
                pe.wait_ge(s_naf, 3 * KD + KD)
                pe.wait_ge(s_router, 32)
                for t in range(NT):
                    b = bank[4][:, t * NE:(t + 1) * NE]
                    for k in range(KD):
                        mm(b, hf[:, k, t * P:(t + 1) * P], rw[:, k, :], start=(k == 0), stop=False)
                    last = mm(b, ones[0:1, :], rb[0:1, :], start=False, stop=True)
                last.then_inc(s_lg, 1)
                for t in range(NT):
                    for i in range(2):
                        if t == 2:
                            pe.wait_ge((s_hna, s_hnv)[i], 1)
                        for k in range(4):
                            d = 4 * i + k
                            last = tr(bank[2 * (t % 2) + i][:, k * P:(k + 1) * P], hf[:, d, t * P:(t + 1) * P], ident)
                        last.then_inc(s_hnt, 1)
                pe.wait_ge(s_sel, 1)
                sel = rt[:, 10, :, :]
                for t in range(NT):
                    b = bank[5][:, t * NE:(t + 1) * NE]
                    mm(b, tri, sel[:, t, :], start=True, stop=(t == 0))
                    for s in range(t):
                        mm(b, ones, sel[:, s, :], start=False, stop=(s == t - 1))
                for t in range(NT):
                    last = mm(bank[6][:, 0:NE], ones, sel[:, t, :], start=(t == 0), stop=(t == NT - 1))
                last.then_inc(s_posd, 1)

            def gather(e, ns, banks):
                w = ns * P
                sets = gather_sets(ns, banks)
                pe.wait_ge(s_oh, e + 1)
                for j, (chunks, at) in enumerate(sets):
                    if j >= len(banks):
                        pe.wait_ge(s_gv, e * KD + sets[j - len(banks)][0][-1] + 1)
                    for i, k in enumerate(chunks):
                        for t in range(NT):
                            last = mm(bank[at][:, i * w:(i + 1) * w], h_nat[:, t, k * P:(k + 1) * P],
                                      onehot[:, t, 0:w], start=(t == 0), stop=(t == NT - 1))
                    last.then_inc(s_gd, len(chunks))

            def turn_gates(e, ns, banks):
                pe.wait_ge(s_gv, e * KD + KD)
                for s in range(ns):
                    if s >= len(banks):
                        pe.wait_ge(s_gtk, e * ITEM + s * (ITEM // ns))
                    for t in range(NT):
                        last = tr(bank[banks[s % len(banks)]][:, t * P:(t + 1) * P],
                                  gated[:, t, s * P:(s + 1) * P], ident)
                    last.then_inc(s_gt, ITEM // ns)

            def scatter(e, ns, odd):
                pe.wait_ge(S["y_act"], e + 2)
                pe.wait_ge(S["y_dve"], e + 2)
                for d in range(KD):
                    if d >= 4:
                        pe.wait_ge(S["x_add"], e * KD + KD + d - 3)
                    for s in range(ns):
                        last = mm(bank[4 + d % 4][:, 0:N], y_sb[:, s, d * P:(d + 1) * P],
                                  gatedT[odd][:, s, :], start=(s == 0), stop=(s == ns - 1))
                    last.then_inc(S["back"], 1)

            for l in range(DEPTH):
                ada(l)
                norm(2 * l)
                projections(l)
                attention(l)
                pooling(l)
                output(l)
                norm(2 * l + 1)
                if l == 0:
                    for k in range(KD):
                        pe.wait_ge(s_nh, 1 * KD + k + 1)
                    dense()
            routing()
            pe.wait_ge(s_route, 1)
            pe.wait_ge(s_hna, NT)
            pe.wait_ge(s_hnv, NT)

            def first_gather(ns):
                gather(0, ns, gather_banks(1))
                turn_gates(0, ns, gather_banks(1))

            by_count(pe, slice(0, 1), first_gather)

            def expert(turn, q, ns):
                e = 2 * turn - 2 + q
                pe.wait_ge(s_gtk, e * ITEM + ITEM)
                last_down = feed_forward(e + 1, F0[1] + q * FF_UNITS, turn, ns)

                def then(ns_next):
                    if ns_next:
                        gather(e + 1, ns_next, gather_banks(ns))
                    last_down()
                    if ns_next:
                        turn_gates(e + 1, ns_next, gather_banks(ns))
                    scatter(e, ns, q)

                by_count(pe, e + 1, then, none=True)

            with pe.Fori(1, NE // 2 + 1) as turn:
                for q in range(2):
                    by_count(pe, 2 * turn - 2 + q, lambda ns: expert(turn, q, ns))
            pe.wait_ge(S["x_add"], NE * KD + KD)
            for t in range(NT):
                for i in range(2):
                    for k in range(4):
                        last = tr(bank[2 * t + i][:, k * P:(k + 1) * P], xT[:, 4 * i + k, t * P:(t + 1) * P], ident)
                    last.then_inc(s_yt, 1)

        @blockctx.scalar
        def _(act):
            A = nc.scalar.activation
            steps = [0]

            def step(ins):
                steps[0] += 1
                ins.then_inc(s_act, 1)
                act.wait_ge(s_act, steps[0])

            act.dma_start(x_nat[:, 0, :], x_prompt[0]).then_inc(s_x, 16)
            act.dma_start(x_nat[:, 1:NT, :], x_sample[0].rearrange("(t p) d -> p t d", p=P)).then_inc(s_x, 16)
            act.dma_start(const[:], const_tab).then_inc(s_const, 16)
            n_mod = DEPTH * MODS
            for dst, src in (
                    (rows[0:n_mod, 0, :], ada_b.rearrange("l (r c) -> (l r) c", c=P)),
                    (rows[n_mod:n_mod + DEPTH * KD, 0, :], norm1_w.rearrange("l (r c) -> (l r) c", c=P)),
                    (rows[n_mod + DEPTH * KD:P, 0, :], norm2_w.rearrange("l (r c) -> (l r) c", c=P)),
                    (rows[R_CTX:R_CTX + KD, 1, :], c_ctx.rearrange("(r c) -> r c", c=P)),
                    (rows[R_C:R_C + KD, 1, :], c[0].rearrange("(r c) -> r c", c=P)),
                    (rows[R_PS:R_QN, 1, :], pool_scale.rearrange("l (r c) -> (l r) c", c=P)),
                    (rows[R_QN:R_KN, 1, 0:HD], q_norm_w), (rows[R_QN:R_KN, 1, HD:P], q_norm_w),
                    (rows[R_KN:R_END, 1, 0:HD], k_norm_w), (rows[R_KN:R_END, 1, HD:P], k_norm_w)):
                act.dma_start(dst, src).then_inc(s_rows, 16)
            act.dma_start(mtab, mix_tab).then_inc(s_mtab, 16)
            act.dma_start(pw, pool_w.rearrange("l g c d -> c (l g) d")).then_inc(s_pw, 16)
            kcv = kc_nat.rearrange("p l (g r n) -> p l g r n", g=N_KV, r=2)
            for l in range(DEPTH):
                for r in range(2):
                    act.dma_start(kcv[:, l, :, r, :], cache_k[0, l]).then_inc(s_cache, 16)
                act.dma_start(vc[:, l, :], cache_v[0, l].rearrange("s g n -> s (g n)")).then_inc(s_cache, 16)
            act.dma_start(rw[:], router_w[0].rearrange("(k p) n -> p k n", p=P)).then_inc(s_router, 16)
            act.dma_start(rb[:], router_b).then_inc(s_router, 16)

            for k in range(0, KD, 2):
                act.wait_ge(s_xt, k + 1)
                A(xT[:, k, :], bank[k][:, 0:N], ACT.Copy).then_inc(s_xa, 1)
            act.wait_ge(s_cols, 2)
            act.wait_ge(s_c0, 1)
            A(cond32[:, :, 0], cols[:, 1, R_CTX:R_CTX + KD], ACT.Silu)
            A(cond32[:, :, 1], cols[:, 1, R_C:R_C + KD], ACT.Silu).then_inc(s_cond, 1)

            def ada(l):
                for u in range(ADA_UNITS):
                    act.wait_ge(s_ada[l], u + 1)
                    if u >= 2:
                        act.wait_ge(s_apm[l], u - 1)
                    A(ada_part[:, u % 2, :], bank[4 + u % 2][:, 0:UCOLS], ACT.Copy).then_inc(s_apk[l], 1)

            def hi(i, freed, turns=0):
                wait_unit(act, i, turns)
                if freed:
                    act.wait_ge(*freed)
                A(hi_of(i), slot(i), ACT.Copy).then_inc(s_hi[split_no(i) % SPLIT], 1)

            def mix_hi(l, u):
                def used(l, v):
                    if v < 0:
                        return (S["first"], GROUPS) if v == -3 else ((S["up"], S["down"])[v + 2], ITEM * GROUPS)
                    return (s_proj[l], min(2 * v + 2, NQK + NG + 1)) if v < 6 else (s_wo[l], 2 * (v - 6) + 2)
                hi(M0[l] + u, used(l, u - 3) if u >= 3 or l == 1 else None)

            def norm(n):
                for k in range(KD):
                    if n == 0:
                        if k == 0:
                            act.wait_ge(s_xa, KD // 2)
                            act.wait_ge(s_xv, KD // 2)
                    elif n % 2 == 1:
                        act.wait_ge(s_x1[n // 2], k + 1)
                    else:
                        act.wait_ge(S["x_add"], k + 1)
                    A(hf[:, k, :], xT[:, k, :], ACT.Square).then_inc(s_nsq, 1)
                act.wait_ge(s_nvar, n + 1)
                A(rstd[:], rstd[:], ACT.Sqrt).then_inc(s_nstd, 1)
                sh = 0 if n % 2 == 0 else 3 * KD
                for k in range(KD + 1):
                    if k < KD:
                        act.wait_ge(s_nt, n * KD + k + 1)
                        for q, (a, b) in enumerate(SEQS):
                            last = A(hf[:, k, a:b], hf[:, k, a:b], ACT.Identity,
                                     bias=mod[:, n // 2, sh + k, q:q + 1], scale=scale_n[:, n, k, q:q + 1])
                        last.then_inc(s_naf, 1)
                    if k >= 1 and n < 3:
                        act.wait_ge(s_naf, n * KD + k)
                        A(a_hi[:, k - 1, :], hf[:, k - 1, :], ACT.Copy).then_inc(s_nhi, 1)

            def projections(l):
                for u in range(2):
                    mix_hi(l, u + 1)
                for j in range(NQK + 1):
                    if j < NQK:
                        act.wait_ge(s_proj[l], j + 1)
                        if j >= 3:
                            act.wait_ge(s_qn[l], j - 2)
                            act.wait_ge(s_ss[l], j - 2)
                        A(raw[:, j % 3, :], bank[j % 3][:, 0:N], ACT.Copy).then_inc(s_raw[l], 1)
                        A(sq[:, j % 3, :], bank[j % 3][:, 0:N], ACT.Square).then_inc(s_sq[l], 1)
                    if j >= 1:
                        act.wait_ge(s_var[l], j)
                        A(hr[:, (j - 1) % 2, :], hr[:, (j - 1) % 2, :], ACT.Sqrt).then_inc(s_std[l], 1)
                    if j in (1, 3, 5):
                        mix_hi(l, 3 + j // 2)
                act.wait_ge(s_pad, 1)
                for g in range(NG):
                    act.wait_ge(s_proj[l], NQK + g + 1)
                    for (a, b), at in zip(SEQS, PADDED):
                        last = A(upad[:, g, at:at + b - a], bank[(NQK + g) % 3][:, a:b], ACT.Copy)
                    last.then_inc(s_u[l], 1)
                act.wait_ge(s_proj[l], NQK + NG + 1)
                A(vT, bank[(NQK + NG) % 3][:, 0:N], ACT.Copy).then_inc(s_vT[l], 1)
                act.wait_ge(s_vn[l], 1)
                A(v_new, bank[0][:, 0:NT * KV_W].rearrange("p (t n) -> p t n", t=NT), ACT.Copy).then_inc(s_v[l], 1)
                act.wait_ge(s_kct[l], 1)
                A(kcT, bank[4][:, 0:N_KV * PAST].rearrange("p (g n) -> p g n", g=N_KV), ACT.Copy).then_inc(s_kck[l], 1)
                act.wait_ge(s_v[l], 1)
                act.dma_start(new_v[0, l].rearrange("s g n -> s (g n)"), v_new[:, 0, :]).then_inc(s_kv[l], 16)
                act.wait_ge(s_kn[l], 1)
                act.dma_start(new_k[0, l], k_nat[:, :, 0:HD]).then_inc(s_kv[l], 16)
                for u in range(3):
                    mix_hi(l, 6 + u)

            def attention(l):
                for s in range(NU + 4):
                    if s < NU:
                        n = N_PROMPT if UNITS[s][0] == 0 else N_SAMPLE + PAST
                        act.wait_ge(s_mx[l], s + 1)
                        if s >= 3:
                            act.wait_ge(s_pt[l], s - 2)
                        A(probs[:, s % 3, 0:n], bank[s % 3][:, 0:n], ACT.Exp, bias=att[:, s % 3, 1:2],
                          scale=HD ** -0.5, accum_out=att[:, s % 3, 2:3]).then_inc(s_ex[l], 1)
                    i = s - 2
                    if 0 <= i < NU:
                        n = N_PROMPT if UNITS[i][0] == 0 else N_SAMPLE + PAST
                        act.wait_ge(s_pt[l], i + 1)
                        if i >= 2:
                            act.wait_ge(s_pv[l], i - 1)
                        A(probsT[:, i % 2, 0:n], bank[3 + i % 2][:, 0:n], ACT.Copy).then_inc(s_ptk[l], 1)
                    i = s - 4
                    if i >= 0 and i % 2 == 1:
                        t, h = UNITS[i]
                        act.wait_ge(s_pv[l], i + 1)
                        A(a_hi[:, h // 2, t * P:(t + 1) * P], bank[5 + i // 2 % 2][:, 0:P], ACT.Copy
                          ).then_inc(s_ah[l], 1)

            def pooling(l):
                for g in range(NG):
                    act.wait_ge(s_pool_mm[l], g + 1)
                    A(a_hi[:, NQ + g, :], bank[g % 2][:, 0:N], ACT.Copy,
                      scale=cols[:, 1, R_PS + l * NG + g:R_PS + l * NG + g + 1]).then_inc(s_pool_hi[l], 1)

            def group_hi(part, F, turns, g, kind):
                if kind < 2:
                    freed = (S["first"], part * GROUPS + g) if kind == 0 else (S["up"], item(part, g, -1, 1))
                else:
                    freed = (S["down"], item(part, g, -1, 1))
                if isinstance(part, int) and g == 0:
                    freed = (s_wo[0], (4, 6, 8)[kind])
                hi(unit(F, g, kind), freed, turns)

            def feed_forward(part, F, turns, ns, groups=range(GROUPS), after_silu=None):
                n = ITEM // ns
                for g in groups:
                    alone = ns == 1 and g == GROUPS - 1
                    for s in range(ns):
                        if s == ns - 1 and g + 1 < GROUPS:
                            group_hi(part, F, turns, g + 1, 0)
                        act.wait_ge(S["up"], item(part, g, s, ns))
                        A(silu_h, bank[0][:, 0:UCOLS], ACT.Silu).then_inc(S["silu"], n)
                        if s == ns - 1 and g + 1 < GROUPS:
                            group_hi(part, F, turns, g + 1, 1)
                        if s == ns - 1 and g == GROUPS - 1 and after_silu:
                            after_silu()
                        if s == 0 and not alone:
                            group_hi(part, F, turns, g, 2)
                        act.wait_ge(S["tr"], item(part, g, s, ns))
                        A(g_hi[:], bank[1][:, 0:UCOLS].rearrange("p (f n) -> p f n", f=2), ACT.Copy
                          ).then_inc(S["g_hi"], n)
                    if alone:
                        group_hi(part, F, turns, g, 2)

            def keep_y(part, ns):
                act.wait_ge(S["down"], item(part, GROUPS - 1, ns - 1, ns))
                for s in range(ns):
                    last = A(y_sb[:, s, 0:512], bank[6 - 2 * s][:, :], ACT.Copy)
                last.then_inc(S["y_act"], 1)

            for l in range(DEPTH):
                ada(l)
                mix_hi(l, 0)
                act.wait_ge(s_mod[l], 1)
                norm(2 * l)
                projections(l)
                attention(l)
                pooling(l)
                act.wait_ge(s_wo[l], 2)
                mix_hi(l, 9)
                norm(2 * l + 1)
                act.wait_ge(s_kv[l], 32)
                if l == 0:
                    group_hi(0, F0[0], 0, 0, 0)
                    group_hi(0, F0[0], 0, 0, 1)
                    feed_forward(0, F0[0], 0, NT)
                    keep_y(0, NT)
            for t in range(NT):
                act.wait_ge(s_hnt, 2 * t + 1)
                A(h_nat[:, t, 0:512], bank[2 * (t % 2)][:, :], ACT.Copy).then_inc(s_hna, 1)
            act.wait_ge(s_dl, 1)
            A(rsmall[:, 3, :], rsmall[:, 2, :], ACT.Exp).then_inc(s_ed, 1)
            act.wait_ge(s_route, 1)

            act.wait_ge(s_wo[1], KD)

            def gathered(e, ns, banks, middle=None):
                sets = gather_sets(ns, banks)
                for j, (chunks, at) in enumerate(sets):
                    if middle and j == len(sets) // 2:
                        middle()
                    n = len(chunks)
                    act.wait_ge(s_gd, e * KD + chunks[-1] + 1)
                    A(a_hi[:, chunks[0]:chunks[-1] + 1, 0:ns * P],
                      bank[at][:, 0:n * ns * P].rearrange("p (k n) -> p k n", k=n), ACT.Copy).then_inc(s_ga, n)

            def keep_gates(e, ns, banks, odd):
                for s in range(ns):
                    act.wait_ge(s_gt, e * ITEM + (s + 1) * (ITEM // ns))
                    A(gatedT[odd][:, s, :], bank[banks[s % len(banks)]][:, 0:N], ACT.Copy
                      ).then_inc(s_gtk, ITEM // ns)

            def first_gathered(ns):
                gathered(0, ns, gather_banks(1))
                keep_gates(0, ns, gather_banks(1), 0)

            group_hi(1, F0[1], 0, 0, 0)
            group_hi(1, F0[1], 0, 0, 1)
            by_count(act, slice(0, 1), first_gathered)

            def expert(turn, q, ns):
                e = 2 * turn - 2 + q
                F = F0[1] + q * FF_UNITS
                feed_forward(e + 1, F, turn, ns, range(GROUPS - 1))

                def then(ns_next):
                    def next_unit(kind):
                        group_hi(e + 2, F + FF_UNITS, turn, 0, kind)

                    feed_forward(e + 1, F, turn, ns, (GROUPS - 1,), ns_next and (lambda: next_unit(0)))
                    if ns_next:
                        gathered(e + 1, ns_next, gather_banks(ns), lambda: next_unit(1))
                    keep_y(e + 1, ns)
                    if ns_next:
                        keep_gates(e + 1, ns_next, gather_banks(ns), 1 - q)

                by_count(act, e + 1, then, none=True)

            with act.Fori(1, NE // 2 + 1) as turn:
                for q in range(2):
                    by_count(act, 2 * turn - 2 + q, lambda ns: expert(turn, q, ns))
            for t in range(NT):
                act.wait_ge(s_yt, 2 * t + 1)
                A(y_sb[:, t, 0:512], bank[2 * t][:, :], ACT.Copy).then_inc(s_ya, 1)

        @blockctx.gpsimd
        def _(pool):
            steps = [0]

            def step(ins):
                steps[0] += 1
                ins.then_inc(s_pool, 1)
                pool.wait_ge(s_pool, steps[0])

            pool.memset(cond32[:], 0.0).then_inc(s_c0, 1)
            pool.memset(win, 0.0)
            pool.memset(upad, 0.0).then_inc(s_pad, 1)
            tt = nc.gpsimd.tensor_tensor
            for l in range(DEPTH):
                if l == 0:
                    pool.wait_ge(s_mtab, 16)
                for j in range(NQK):
                    pool.wait_ge(s_qn[l], j + 1)
                    if j >= 2:
                        pool.wait_ge(s_qk[l], j - 1)
                    tt(rope_a[:, j % 2, :], qn[:, j, N_PROMPT:N], mtab[:, M_COS:M_COS + N_SAMPLE],
                       ALU.mult).then_inc(s_ra[l], 1)
                for g, w in enumerate(WINDOWS):
                    pool.wait_ge(s_u[l], g + 1)
                    u = upad[:, g, :]
                    lo, hi = 1, PADW
                    step(tt(win[:, 0, lo:hi], u[:, lo - 1:hi - 1], u[:, lo:hi], ALU.add))
                    at, n = 0, 2
                    while n < w:
                        h = n // 2
                        lo, hi = lo + h, hi - h
                        step(tt(win[:, 1 - at, lo:hi], win[:, at, lo - h:hi - h],
                                win[:, at, lo + h:hi + h], ALU.add))
                        at, n = 1 - at, 2 * n
                    for (a, b), p in zip(SEQS, PADDED):
                        last = tt(win[:, 1 - at, p:p + b - a], win[:, at, p:p + b - a],
                                  mtab[:, M_INV + g * N + a:M_INV + g * N + b], ALU.mult)
                    step(last)
                    for (a, b), p in zip(SEQS, PADDED):
                        last = tt(diff[:, g, a:b], win[:, 1 - at, p:p + b - a], u[:, p:p + b - a],
                                  ALU.subtract)
                    last.then_inc(s_d[l], 1)
                    pool.wait_ge(s_d[l], g + 1)

        @blockctx.vector
        def _(dve):
            V = nc.vector
            steps = [0]

            def step(ins):
                steps[0] += 1
                ins.then_inc(s_dve, 1)
                dve.wait_ge(s_dve, steps[0])

            for k in range(1, KD, 2):
                dve.wait_ge(s_xt, k + 1)
                V.tensor_copy(xT[:, k, :], bank[k][:, 0:N]).then_inc(s_xv, 1)
            dve.wait_ge(s_colsT, 1)
            V.tensor_copy(cols[:, 0, :], bank[0][:, 0:P]).then_inc(s_cols, 1)
            V.tensor_copy(cols[:, 1, 0:R_END], bank[1][:, 0:R_END]).then_inc(s_cols, 1)
            dve.wait_ge(s_cols, 2)

            def modulation(l):
                dve.wait_ge(s_apm[l], ADA_UNITS)
                step(V.tensor_tensor(mod[:, l, :, :], bank[3][:, 0:2 * MODS].rearrange("p (m c) -> p m c", c=2),
                                     adab(l).unsqueeze(2).to_broadcast((P, MODS, 2)), ALU.add))
                for i in range(2):
                    sc = (1 + 3 * i) * KD
                    last = V.scalar_tensor_tensor(scale_n[:, 2 * l + i], mod[:, l, sc:sc + KD, :], 1.0,
                                                  normw(2 * l + i).unsqueeze(2).to_broadcast((P, KD, 2)),
                                                  ALU.add, ALU.mult)
                last.then_inc(s_mod[l], 1)
                dve.wait_ge(s_mod[l], 1)

            def norm(n):
                dve.wait_ge(s_nss, n + 1)
                V.tensor_scalar(rstd[:], bank[0][:, 0:N], 1.0 / D, EPS, ALU.mult, ALU.add).then_inc(s_nvar, 1)
                dve.wait_ge(s_nstd, n + 1)
                step(V.reciprocal(rstd[:], rstd[:]))
                for k in range(KD):
                    V.tensor_tensor(hf[:, k, :], xT[:, k, :], rstd[:], ALU.mult).then_inc(s_nt, 1)
                if n < 3:
                    for k in range(KD):
                        dve.wait_ge(s_nhi, n * KD + k + 1)
                        V.tensor_tensor(a_lo[:, k, :], hf[:, k, :], a_hi[:, k, :].bitcast(f32), ALU.subtract
                                        ).then_inc(s_nh, 1)

            def lo(i, turns=0):
                dve.wait_ge(*split_count(s_hi, i, turns))
                V.tensor_tensor(lo_of(i), slot(i), hi_of(i).bitcast(f32), ALU.subtract
                                ).then_inc(s_lo[split_no(i) % SPLIT], 1)

            def projections(l):
                dve.wait_ge(s_mtab, 16)
                for u in range(2):
                    lo(M0[l] + u + 1)
                for j in range(NQK + 2):
                    if j < NQK:
                        dve.wait_ge(s_ss[l], j + 1)
                        if j >= 2:
                            dve.wait_ge(s_qn[l], j - 1)
                        V.tensor_scalar(hr[:, j % 2, :], bank[3 + j % 2][:, 0:N], 1.0 / HD, EPS,
                                        ALU.mult, ALU.add).then_inc(s_var[l], 1)
                    i = j - 1
                    if 0 <= i < NQK:
                        dve.wait_ge(s_std[l], i + 1)
                        step(V.reciprocal(hr[:, i % 2, :], hr[:, i % 2, :]))
                        dve.wait_ge(s_raw[l], i + 1)
                        w = (R_QN if i < NQ else R_KN) + l
                        V.scalar_tensor_tensor(qn[:, i, :], raw[:, i % 3, :], cols[:, 1, w:w + 1], hr[:, i % 2, :],
                                               ALU.mult, ALU.mult).then_inc(s_qn[l], 1)
                    if j in (2, 4, 6):
                        lo(M0[l] + 2 + j // 2)
                    i = j - 2
                    if 0 <= i < NQK:
                        dve.wait_ge(s_rot[l], i + 1)
                        step(V.tensor_tensor(rope_b[:, i % 2, :], bank[5 + i % 2][:, 0:N_SAMPLE],
                                             mtab[:, M_SIN:M_SIN + N_SAMPLE], ALU.mult))
                        dve.wait_ge(s_ra[l], i + 1)
                        V.tensor_tensor(qn[:, i, N_PROMPT:N], rope_a[:, i % 2, :], rope_b[:, i % 2, :],
                                        ALU.add).then_inc(s_qk[l], 1)
                dve.wait_ge(s_kt[l], 1)
                V.tensor_copy(k_nat[:], bank[3][:, 0:N_KV * P].rearrange("p (g n) -> p g n", g=N_KV)
                              ).then_inc(s_kn[l], 1)
                for u in range(3):
                    lo(M0[l] + 6 + u)

            def attention(l):
                for s in range(NU + 4):
                    if s < NU:
                        n = N_PROMPT if UNITS[s][0] == 0 else N_SAMPLE + PAST
                        dve.wait_ge(s_sc[l], s + 1)
                        a = att[:, s % 3, :]
                        step(V.reduce_max(a[:, 0:1], bank[s % 3][:, 0:n], AX.X))
                        V.tensor_scalar(a[:, 1:2], a[:, 0:1], -HD ** -0.5, None, ALU.mult).then_inc(s_mx[l], 1)
                    i = s - 1
                    if 0 <= i < NU:
                        n = N_PROMPT if UNITS[i][0] == 0 else N_SAMPLE + PAST
                        dve.wait_ge(s_ex[l], i + 1)
                        a = att[:, i % 3, :]
                        step(V.reciprocal(a[:, 3:4], a[:, 2:3]))
                        V.tensor_scalar(probs[:, i % 3, 0:n], probs[:, i % 3, 0:n], a[:, 3:4], None,
                                        ALU.mult).then_inc(s_pn[l], 1)
                    i = s - 4
                    if i >= 0 and i % 2 == 1:
                        t, h = UNITS[i]
                        dve.wait_ge(s_ah[l], i // 2 + 1)
                        c_ = (h // 2, slice(t * P, (t + 1) * P))
                        V.tensor_tensor(a_lo[:, c_[0], c_[1]], bank[5 + i // 2 % 2][:, 0:P],
                                        a_hi[:, c_[0], c_[1]].bitcast(f32), ALU.subtract).then_inc(s_av[l], 1)

            def pooling(l):
                for g in range(NG):
                    dve.wait_ge(s_pool_hi[l], g + 1)
                    w = R_PS + l * NG + g
                    V.scalar_tensor_tensor(a_lo[:, NQ + g, :], bank[g % 2][:, 0:N], cols[:, 1, w:w + 1],
                                           a_hi[:, NQ + g, :].bitcast(f32), ALU.mult, ALU.subtract
                                           ).then_inc(s_pooled[l], 1)

            def add_x(src, ready, first, g, l, done):
                for d in range(KD):
                    dve.wait_ge(ready, first + d + 1)
                    for q, (a, b) in enumerate(SEQS):
                        last = V.scalar_tensor_tensor(xT[:, d, a:b], src(d)[:, a:b], mod[:, l, g + d, q:q + 1],
                                                      xT[:, d, a:b], ALU.mult, ALU.add)
                    last.then_inc(done, 1)

            def feed_forward(part, F, turns, ns, groups=range(GROUPS), halfway=None, after_mul=None):
                n = ITEM // ns
                for g in groups:
                    alone = ns == 1 and g == GROUPS - 1
                    if g == GROUPS // 2 and halfway:
                        halfway()
                    for s in range(ns):
                        if s == ns - 1 and g + 1 < GROUPS:
                            lo(unit(F, g + 1, 0), turns)
                        dve.wait_ge(S["silu"], item(part, g, s, ns))
                        V.tensor_tensor(g_nat, silu_h, bank[0][:, UCOLS:2 * UCOLS], ALU.mult).then_inc(S["mul"], n)
                        if s == ns - 1 and g + 1 < GROUPS:
                            lo(unit(F, g + 1, 1), turns)
                        if s == ns - 1 and g == GROUPS - 1 and after_mul:
                            after_mul()
                        if s == 0 and not alone:
                            lo(unit(F, g, 2), turns)
                        dve.wait_ge(S["g_hi"], item(part, g, s, ns))
                        V.tensor_tensor(g_lo[:], bank[1][:, 0:UCOLS].rearrange("p (f n) -> p f n", f=2),
                                        g_hi[:].bitcast(f32), ALU.subtract).then_inc(S["g_lo"], n)
                    if alone:
                        lo(unit(F, g, 2), turns)

            def keep_y(part, ns):
                dve.wait_ge(S["down"], item(part, GROUPS - 1, ns - 1, ns))
                for s in range(ns):
                    last = V.tensor_copy(y_sb[:, s, 512:D], bank[7 - 2 * s][:, :])
                last.then_inc(S["y_dve"], 1)

            def routing():
                r = lambda i: rt[:, i, :, :]
                m = lambda i: rsmall[:, i, :]
                wide = lambda v: v.unsqueeze(2).to_broadcast((P, NT, NE))
                L, eq, key, sel1, L2, sel2, sel, g1, g2, gate = (r(i) for i in (0, 1, 2, 3, 4, 5, 10, 6, 7, 8))
                rk = rank.unsqueeze(1).to_broadcast((P, NT, NE))
                dve.wait_ge(s_lg, 1)
                step(V.tensor_copy(L, bank[4][:, 0:NT * NE].rearrange("p (t n) -> p t n", t=NT)))
                for t in range(NT):
                    dve.wait_ge(s_hnt, 2 * t + 2)
                    V.tensor_copy(h_nat[:, t, 512:D], bank[2 * (t % 2) + 1][:, :]).then_inc(s_hnv, 1)

                def first_largest(x, largest, out):
                    step(V.reduce_max(largest, x, AX.X))
                    step(V.tensor_tensor(eq, x, wide(largest), ALU.is_equal))
                    step(V.tensor_tensor(key, eq, rk, ALU.mult))
                    step(V.reduce_max(m(5), key, AX.X))
                    step(V.tensor_tensor(out, key, wide(m(5)), ALU.is_equal))

                first_largest(L, m(0), sel1)
                step(V.scalar_tensor_tensor(L2, sel1, -3.0e38, L, ALU.mult, ALU.add))
                first_largest(L2, m(1), sel2)
                V.tensor_tensor(sel, sel1, sel2, ALU.add).then_inc(s_sel, 1)
                V.tensor_tensor(m(2), m(1), m(0), ALU.subtract).then_inc(s_dl, 1)
                dve.wait_ge(s_ed, 1)
                step(V.tensor_scalar(m(4), m(3), 1.0, None, ALU.add))
                step(V.reciprocal(m(6), m(4)))
                step(V.tensor_tensor(m(7), m(6), m(3), ALU.mult))
                V.tensor_tensor(g1, sel1, wide(m(6)), ALU.mult)
                step(V.tensor_tensor(g2, sel2, wide(m(7)), ALU.mult))
                by_expert = lambda i: route[:, 0:NE, i, :].rearrange("p e t -> p t e")
                V.tensor_tensor(by_expert(1), g1, g2, ALU.add)
                dve.wait_ge(s_sel, 1)
                dve.wait_ge(s_posd, 1)
                step(V.scalar_tensor_tensor(r(9), bank[5][:, 0:NT * NE].rearrange("p (t n) -> p t n", t=NT), 1.0,
                                            sel, ALU.add, ALU.mult))
                V.tensor_scalar(by_expert(0), r(9), -1.0, None, ALU.add)
                V.memset(counts[:, NE:NE + 1], N + 1)
                V.memset(route[:, NE, :, :], 0.0)
                V.tensor_copy(counts[:, 0:NE], bank[6][0:1, 0:NE]).then_inc(s_route, 1)
                dve.wait_ge(s_route, 1)

            def one_hot(e, now):
                V.tensor_copy(cur[:].rearrange("p (o i t) -> p o i t", o=1, i=2), route[:, now, :, :]
                              ).then_inc(s_cur, 1)
                dve.wait_ge(s_cur, e + 1)
                for t in range(NT):
                    V.tensor_scalar(onehot[:, t, :], iota, cur[:, t:t + 1], None, ALU.is_equal)
                for t in range(NT):
                    last = V.tensor_scalar(gated[:, t, :], iota, cur[:, t:t + 1],
                                           cur[:, NT + t:NT + t + 1], ALU.is_equal, ALU.mult)
                last.then_inc(s_oh, 1)

            def gathered(e, ns, banks, middle=None):
                sets = gather_sets(ns, banks)
                for j, (chunks, at) in enumerate(sets):
                    if middle and j == len(sets) // 2:
                        middle()
                    n, k = len(chunks), slice(chunks[0], chunks[-1] + 1)
                    dve.wait_ge(s_ga, e * KD + chunks[-1] + 1)
                    V.tensor_tensor(a_lo[:, k, 0:ns * P], bank[at][:, 0:n * ns * P].rearrange("p (k n) -> p k n", k=n),
                                    a_hi[:, k, 0:ns * P].bitcast(f32), ALU.subtract).then_inc(s_gv, n)

            def expert(turn, q, ns):
                e = 2 * turn - 2 + q
                F = F0[1] + q * FF_UNITS

                def next_one_hot():
                    dve.wait_ge(s_gt, e * ITEM + ITEM)
                    one_hot(e + 1, ds(e + 1, 1))

                feed_forward(e + 1, F, turn, ns, range(GROUPS - 1), halfway=next_one_hot)

                def then(ns_next):
                    feed_forward(e + 1, F, turn, ns, (GROUPS - 1,),
                                 after_mul=ns_next and (lambda: lo(F + FF_UNITS, turn)))
                    if ns_next:
                        gathered(e + 1, ns_next, gather_banks(ns), lambda: lo(F + FF_UNITS + 1, turn))
                    keep_y(e + 1, ns)
                    dve.wait_ge(S["x_add"], e * KD + KD)
                    add_x(lambda d: bank[4 + d % 4], S["back"], e * KD + KD, 5 * KD, 1, S["x_add"])

                by_count(dve, e + 1, then, none=True)

            for l in range(DEPTH):
                modulation(l)
                lo(M0[l])
                norm(2 * l)
                projections(l)
                attention(l)
                pooling(l)
                lo(M0[l] + 9)
                add_x(lambda d: bank[2 + d % 4], s_wo[l], 0, 2 * KD, l, s_x1[l])
                norm(2 * l + 1)
                dve.wait_ge(s_kv[l], 32)
                if l == 0:
                    lo(F0[0])
                    lo(F0[0] + 1)
                    feed_forward(0, F0[0], 0, NT)
                    keep_y(0, NT)
                    add_x(lambda d: bank[4 + d % 4], S["back"], 0, 5 * KD, 0, S["x_add"])
            routing()
            one_hot(0, slice(0, 1))
            lo(F0[1])
            by_count(dve, slice(0, 1), lambda ns: gathered(0, ns, gather_banks(1)))
            lo(F0[1] + 1)
            with dve.Fori(1, NE // 2 + 1) as turn:
                for q in range(2):
                    by_count(dve, 2 * turn - 2 + q, lambda ns: expert(turn, q, ns))
            for t in range(NT):
                dve.wait_ge(s_yt, 2 * t + 2)
                V.tensor_copy(y_sb[:, t, 512:D], bank[2 * t + 1][:, :]).then_inc(s_yv, 1)


_INS = ("x_prompt", "x_sample", "cache_k", "cache_v", "c", "c_ctx", "norm1_w", "norm2_w", "ada_w", "ada_b",
        "w_in", "w_o", "q_norm_w", "k_norm_w", "pool_w", "pool_scale", "ffn_w1", "ffn_w3", "ffn_w2",
        "router_w", "router_b", "moe_w1", "moe_w3", "moe_w2")
_OUTS = ((1, N_PROMPT, D), (1, N_SAMPLE, D), (1, DEPTH, N_PROMPT, N_KV, HD), (1, DEPTH, N_PROMPT, N_KV, HD))


def kernel(**inputs):
    import concourse.bacc as bacc
    from concourse.bass_utils import run_bass_kernel_spmd

    nc = bacc.Bacc("TRN2", target_bir_lowering=False, num_devices=1)
    arrays, args = {}, []
    tables = dict(zip(("const_tab", "mix_tab"), constants()))
    for name in _INS + tuple(tables):
        a = np.ascontiguousarray(tables[name] if name in tables else inputs[name])
        arrays[f"in_{name}"] = a
        args.append(nc.dram_tensor(f"in_{name}", a.shape, mybir.dt.from_np(a.dtype), kind="ExternalInput").ap())
    for i, shape in enumerate(_OUTS):
        args.append(nc.dram_tensor(f"out_{i}", shape, mybir.dt.float32, kind="ExternalOutput").ap())
    build(nc, *args)
    r = run_bass_kernel_spmd(nc, [arrays], core_ids=[0])
    return tuple(r.results[0][f"out_{i}"] for i in range(len(_OUTS)))
```
